# Optimizing a Trainium2 kernel written in Bass

```python
import jax, jax.numpy as jnp
from jax import lax
import numpy as np

D_MODEL = 1024
BATCH = 1
SEQ = 512
DEPTH = 1

HEAD_DIM = 64
DSA_HEADS = 8
DSA_Q_RANK = 256
DSA_KV_RANK = 128
IDX_HEADS = 4
IDX_DIM = 64
DSA_TOPK_MAX = 256
MOBA_HEADS = 8
MOBA_BLOCK = 256
MOBA_TOPK = 3
D_FF = 2816
N_MOD = 9
DSA_Q_CHUNK = 128
MOBA_Q_CHUNK = 16
EPS = 1e-6
DSA_WIDTH = DSA_HEADS * HEAD_DIM
MOBA_WIDTH = MOBA_HEADS * HEAD_DIM
IN_SPLITS = (DSA_Q_RANK, DSA_KV_RANK, IDX_DIM, IDX_HEADS, MOBA_WIDTH, MOBA_WIDTH, MOBA_WIDTH, D_MODEL, D_MODEL)
IN_WIDTH = DSA_Q_RANK + DSA_KV_RANK + IDX_DIM + IDX_HEADS + 3 * MOBA_WIDTH + 2 * D_MODEL

kernel_name = "hybrid_dsa_moba_macaron_adaln"

def rms_norm(x, g):
    xf = x.astype(jnp.float32)
    y = xf * lax.rsqrt(jnp.mean(xf * xf, axis=-1, keepdims=True) + EPS)
    return (y * g.astype(jnp.float32)).astype(x.dtype)

def layer_norm(x, g, b):
    xf = x.astype(jnp.float32)
    mu = jnp.mean(xf, axis=-1, keepdims=True)
    xc = xf - mu
    y = xc * lax.rsqrt(jnp.mean(xc * xc, axis=-1, keepdims=True) + EPS)
    return (y * g.astype(jnp.float32) + b.astype(jnp.float32)).astype(x.dtype)

def alibi_slopes(n):
    return 2.0 ** (-8.0 * (jnp.arange(n, dtype=jnp.float32) + 1.0) / n)

def modulate(h, shift, scale):
    return h * (1.0 + scale[:, None, :]) + shift[:, None, :]

def swiglu(h, w1, w3, w2):
    return (jax.nn.silu(h @ w1) * (h @ w3)) @ w2

def split_cols(p):
    offs, o = [], 0
    for w in IN_SPLITS[:-1]:
        o += w
        offs.append(o)
    return jnp.split(p, offs, axis=-1)

def dsa_attention(cq, ckv, k_idx, w_idx, w_uq, w_qidx, w_uk, w_uv):
    B, S, _ = cq.shape
    k_sel = min(DSA_TOPK_MAX, S // 4)
    qc = min(DSA_Q_CHUNK, S)
    n_chunks = S // qc
    slopes = alibi_slopes(DSA_HEADS)
    scale = HEAD_DIM ** -0.5
    q = jnp.einsum('bsr,rhd->bshd', cq, w_uq)
    q_lat = jnp.einsum('bshd,chd->bshc', q, w_uk) * scale
    q_idx = jnp.einsum('bsr,rhd->bshd', cq, w_qidx)
    w_idx = w_idx * (IDX_HEADS ** -0.5 * IDX_DIM ** -0.5)
    key_pos = jnp.arange(S)

    def chunked(a):
        return a.reshape((B, n_chunks, qc) + a.shape[2:]).swapaxes(0, 1)

    def step(args):
        ci, ql, qi, wi = args
        t = ci * qc + jnp.arange(qc)
        rel = jax.nn.relu(jnp.einsum('bqhd,bsd->bqhs', qi, k_idx))
        score = jnp.einsum('bqhs,bqh->bqs', rel, wi).astype(jnp.float32)
        score = jnp.where(key_pos[None, None, :] <= t[None, :, None], score, -jnp.inf)
        _, idx = lax.top_k(score, k_sel)
        kv = jax.vmap(lambda cc, ii: cc[ii])(ckv, idx)
        s = jnp.einsum('bqhc,bqkc->bqhk', ql, kv).astype(jnp.float32)
        dist = (t[None, :, None] - idx).astype(jnp.float32)
        s = s - slopes[None, None, :, None] * dist[:, :, None, :]
        s = jnp.where((dist >= 0)[:, :, None, :], s, -jnp.inf)
        p = jax.nn.softmax(s, axis=-1).astype(kv.dtype)
        return jnp.einsum('bqhk,bqkc->bqhc', p, kv)

    o_lat = lax.map(step, (jnp.arange(n_chunks), chunked(q_lat), chunked(q_idx), chunked(w_idx)))
    o_lat = o_lat.swapaxes(0, 1).reshape(B, S, DSA_HEADS, DSA_KV_RANK)
    o = jnp.einsum('bshc,chd->bshd', o_lat, w_uv)
    return o.reshape(B, S, DSA_WIDTH)

def moba_attention(q, k, v):
    B, S, H, Dh = q.shape
    nb = -(-S // MOBA_BLOCK)
    pad = nb * MOBA_BLOCK - S
    kp = jnp.pad(k, ((0, 0), (0, pad), (0, 0), (0, 0)))
    vp = jnp.pad(v, ((0, 0), (0, pad), (0, 0), (0, 0)))
    kb = kp.reshape(B, nb, MOBA_BLOCK, H, Dh).transpose(0, 3, 1, 2, 4)
    vb = vp.reshape(B, nb, MOBA_BLOCK, H, Dh).transpose(0, 3, 1, 2, 4)
    k_mean = jnp.mean(kb, axis=3)
    n_top = min(MOBA_TOPK, nb - 1)
    qc = min(MOBA_Q_CHUNK, S)
    n_chunks = S // qc
    slopes = alibi_slopes(MOBA_HEADS)
    scale = Dh ** -0.5
    blk_ids = jnp.arange(nb)
    off = jnp.arange(MOBA_BLOCK)
    gather = jax.vmap(jax.vmap(lambda blocks, ii: blocks[ii]))

    def step(args):
        ci, qq = args
        t = ci * qc + jnp.arange(qc)
        blk = (ci * qc) // MOBA_BLOCK
        k_own = lax.dynamic_slice_in_dim(kp, blk * MOBA_BLOCK, MOBA_BLOCK, axis=1)
        v_own = lax.dynamic_slice_in_dim(vp, blk * MOBA_BLOCK, MOBA_BLOCK, axis=1)
        s_own = jnp.einsum('bqhd,bkhd->bqhk', qq, k_own).astype(jnp.float32) * scale
        d_own = (t[:, None] - (blk * MOBA_BLOCK + off)[None, :]).astype(jnp.float32)
        s_own = s_own - slopes[None, None, :, None] * d_own[None, :, None, :]
        s_own = jnp.where((d_own >= 0)[None, :, None, :], s_own, -jnp.inf)
        if n_top == 0:
            p_own = jax.nn.softmax(s_own, axis=-1).astype(v.dtype)
            return jnp.einsum('bqhk,bkhd->bqhd', p_own, v_own)
        gate = jnp.einsum('bqhd,bhnd->bqhn', qq, k_mean).astype(jnp.float32)
        gate = jnp.where(blk_ids < blk, gate, -jnp.inf)
        _, sel = lax.top_k(gate, n_top)
        sel_h = sel.transpose(0, 2, 1, 3)
        k_sel = gather(kb, sel_h)
        v_sel = gather(vb, sel_h)
        s_past = jnp.einsum('bqhd,bhqjkd->bqhjk', qq, k_sel).astype(jnp.float32) * scale
        d_past = (t[None, :, None, None, None] - (sel[..., None] * MOBA_BLOCK + off)).astype(jnp.float32)
        s_past = s_past - slopes[None, None, :, None, None] * d_past
        s_past = jnp.where((sel < blk)[..., None], s_past, -jnp.inf)
        n_past = n_top * MOBA_BLOCK
        s_all = jnp.concatenate([s_past.reshape(B, qc, H, n_past), s_own], axis=-1)
        p = jax.nn.softmax(s_all, axis=-1).astype(v.dtype)
        p_past = p[..., :n_past].reshape(B, qc, H, n_top, MOBA_BLOCK)
        p_own = p[..., n_past:]
        return (jnp.einsum('bqhjk,bhqjkd->bqhd', p_past, v_sel)
                + jnp.einsum('bqhk,bkhd->bqhd', p_own, v_own))

    qs = q.reshape(B, n_chunks, qc, H, Dh).swapaxes(0, 1)
    o = lax.map(step, (jnp.arange(n_chunks), qs))
    return o.swapaxes(0, 1).reshape(B, S, H * Dh)

def setup_inputs(seed: int = 0) -> dict:
    key = jax.random.key(seed)
    ks = jax.random.split(key, 32)

    def nrm(k, shape, scale):
        return jax.random.normal(k, shape, jnp.float32) * scale

    def gain(k, shape):
        return 1.0 + 0.02 * jax.random.normal(k, shape, jnp.float32)

    L = DEPTH
    return {
        "x": nrm(ks[0], (BATCH, SEQ, D_MODEL), 1.0),
        "c": nrm(ks[1], (BATCH, D_MODEL), 1.0),
        "w_ada": nrm(ks[2], (L, D_MODEL, N_MOD * D_MODEL), 0.1 * D_MODEL ** -0.5),
        "b_ada": nrm(ks[3], (L, N_MOD * D_MODEL), 0.01),
        "g_ffn1": gain(ks[4], (L, D_MODEL)),
        "w1_ffn1": nrm(ks[5], (L, D_MODEL, D_FF), D_MODEL ** -0.5),
        "w3_ffn1": nrm(ks[6], (L, D_MODEL, D_FF), D_MODEL ** -0.5),
        "w2_ffn1": nrm(ks[7], (L, D_FF, D_MODEL), D_FF ** -0.5),
        "g_mix": gain(ks[8], (L, D_MODEL)),
        "w_in": nrm(ks[9], (L, D_MODEL, IN_WIDTH), D_MODEL ** -0.5),
        "g_cq": gain(ks[10], (L, DSA_Q_RANK)),
        "g_ckv": gain(ks[11], (L, DSA_KV_RANK)),
        "g_kidx": gain(ks[12], (L, IDX_DIM)),
        "b_kidx": nrm(ks[13], (L, IDX_DIM), 0.01),
        "w_uq": nrm(ks[14], (L, DSA_Q_RANK, DSA_HEADS, HEAD_DIM), DSA_Q_RANK ** -0.5),
        "w_qidx": nrm(ks[15], (L, DSA_Q_RANK, IDX_HEADS, IDX_DIM), DSA_Q_RANK ** -0.5),
        "w_uk": nrm(ks[16], (L, DSA_KV_RANK, DSA_HEADS, HEAD_DIM), DSA_KV_RANK ** -0.5),
        "w_uv": nrm(ks[17], (L, DSA_KV_RANK, DSA_HEADS, HEAD_DIM), DSA_KV_RANK ** -0.5),
        "w_proj_dsa": nrm(ks[18], (L, DSA_WIDTH, D_MODEL), DSA_WIDTH ** -0.5),
        "w_proj_moba": nrm(ks[19], (L, MOBA_WIDTH, D_MODEL), MOBA_WIDTH ** -0.5),
        "w_out": nrm(ks[20], (L, D_MODEL, D_MODEL), D_MODEL ** -0.5),
        "g_ffn2": gain(ks[21], (L, D_MODEL)),
        "w1_ffn2": nrm(ks[22], (L, D_MODEL, D_FF), D_MODEL ** -0.5),
        "w3_ffn2": nrm(ks[23], (L, D_MODEL, D_FF), D_MODEL ** -0.5),
        "w2_ffn2": nrm(ks[24], (L, D_FF, D_MODEL), D_FF ** -0.5),
        "g_final": gain(ks[25], (D_MODEL,)),
    }

def reference(x, c, w_ada, b_ada, g_ffn1, w1_ffn1, w3_ffn1, w2_ffn1, g_mix, w_in,
              g_cq, g_ckv, g_kidx, b_kidx, w_uq, w_qidx, w_uk, w_uv,
              w_proj_dsa, w_proj_moba, w_out, g_ffn2, w1_ffn2, w3_ffn2, w2_ffn2, g_final):
    B, S, _ = x.shape
    c_act = jax.nn.silu(c)
    for i in range(DEPTH):
        mods = c_act @ w_ada[i] + b_ada[i]
        sh1, sc1, gt1, sh2, sc2, gt2, sh3, sc3, gt3 = jnp.split(mods, N_MOD, axis=-1)

        h = modulate(rms_norm(x, g_ffn1[i]), sh1, sc1)
        x = x + 0.5 * (1.0 + gt1[:, None, :]) * swiglu(h, w1_ffn1[i], w3_ffn1[i], w2_ffn1[i])

        h = modulate(rms_norm(x, g_mix[i]), sh2, sc2)
        cq, ckv, kidx, widx, mq, mk, mv, ga, gb = split_cols(h @ w_in[i])
        cq = rms_norm(cq, g_cq[i])
        ckv = rms_norm(ckv, g_ckv[i])
        kidx = layer_norm(kidx, g_kidx[i], b_kidx[i])
        y_dsa = dsa_attention(cq, ckv, kidx, widx, w_uq[i], w_qidx[i], w_uk[i], w_uv[i]) @ w_proj_dsa[i]
        shp = (B, S, MOBA_HEADS, HEAD_DIM)
        y_moba = moba_attention(mq.reshape(shp), mk.reshape(shp), mv.reshape(shp)) @ w_proj_moba[i]
        y = jax.nn.sigmoid(ga) * y_dsa + jax.nn.sigmoid(gb) * y_moba
        x = x + (1.0 + gt2[:, None, :]) * (y @ w_out[i])

        h = modulate(rms_norm(x, g_ffn2[i]), sh3, sc3)
        x = x + 0.5 * (1.0 + gt3[:, None, :]) * swiglu(h, w1_ffn2[i], w3_ffn2[i], w2_ffn2[i])
    return rms_norm(x, g_final)


_drawn_inputs = setup_inputs


def setup_inputs(seed=0):
    import zlib

    import numpy as np

    out = dict(_drawn_inputs(seed))
    spreads = {}
    factors = {'g_ffn1': 2.668, 'g_ckv': 8.0, 'b_kidx': 2.989, 'g_ffn2': 7.078, 'g_final': 2.799}
    for name, (base, spread) in spreads.items():
        noise = np.random.default_rng([zlib.crc32(name.encode()), seed]).standard_normal(out[name].shape)
        drawn = base * np.exp(spread * noise) if base else spread * noise
        out[name] = __import__('jax').numpy.asarray(drawn.astype(out[name].dtype))
    for name, factor in factors.items():
        out[name] = (out[name] * factor).astype(out[name].dtype)
    return out
```

```python
from contextlib import ExitStack

import concourse.bass as bass
from concourse import mybir

F32 = mybir.dt.float32
F32R = mybir.dt.float32r
ALU = mybir.AluOpType
ACT = mybir.ActivationFunctionType
AX = mybir.AxisListType

P = 128
SEQ = 512
D_MODEL = 1024
D_FF = 2816
HEADS = 8
HEAD_DIM = 64
IDX_HEADS = 4
TOPK = 128
EPS = 1e-6
KD = D_MODEL // P
KF = D_FF // P
KH = KF // 2
QT = SEQ // P
HP = HEADS // 2
N_MOD = 9

RAW = 4
SPL = 2

U_UP = [0, 108]
U_DOWN = [44, 152]
U_LAT = 60
U_QKV = 64
U_GATE = 76
U_MERGE = 92
U_OUT = 100
QKV_COL = 452

R_BADA, R_G1, R_GM, R_G2, R_GF, R_CQ, R_CKV, R_C, R_GK, R_BK = 0, 72, 80, 88, 96, 104, 106, 107, 115, 116
N_ROWS = 117

ADA_FIRST = 20
ADA_DVE = 8
MASKED = -1.0e30
FUTURE = -3.0e38
TAKEN = -3.3e38


def build_layer(nc, x_in, c_in, w_ada, b_ada, g_ffn1, w1_ffn1, w3_ffn1, w2_ffn1, g_mix, w_in, g_cq, g_ckv,
                g_kidx, b_kidx, w_uq, w_qidx, w_uk, w_uv, w_proj_dsa, w_proj_moba, w_out, g_ffn2, w1_ffn2,
                w3_ffn2, w2_ffn2, g_final, out):
    ctx = ExitStack()
    with ctx:
        base = -(-nc.sbuf_base // 64) * 64

        def at(name, shape, offset, dt=F32):
            return nc.alloc_sbuf_tensor_at(name, [P] + shape, dt, offset=base + offset)

        raw = [at(f"raw{r}", [KH * P], r * 5632) for r in range(RAW)]
        w_hi = [at(f"w_hi{r}", [KH * P], 22528 + r * 5632, F32R) for r in range(SPL)]
        w_lo = [at(f"w_lo{r}", [KH * P], 33792 + r * 5632, F32R) for r in range(SPL)]
        xT = at("xT", [KD, SEQ], 45056)
        h_hi = at("h_hi", [KD, SEQ], 61440, F32R)
        h_lo = at("h_lo", [KD, SEQ], 77824, F32R)
        big = 94208
        g_hi = at("g_hi", [KF, SEQ], big, F32R)
        g_lo = at("g_lo", [KF, SEQ], big + 45056, F32R)
        tmp = at("tmp", [4, SEQ], big + 90112)
        nrm = at("nrm", [4, SEQ], big + 81920)
        ada = at("ada", [4, KD, P], big + 98304)
        ada0 = at("ada0", [ADA_FIRST, KD, P], big)
        x_tok = at("x_tok", [QT, D_MODEL], big + 98304)
        dq = at("dq", [HP, SEQ], big)
        dk = at("dk", [HP, SEQ], big + 8192)
        dv = at("dv", [QT, SEQ], big + 16384)
        qi = at("qi", [2, SEQ], big + 24576)
        ki = at("ki", [SEQ], big + 28672)
        score = at("score", [3, SEQ], big + 30720)
        dist = at("dist", [SEQ], big + 36864)
        mq = at("mq", [HP, SEQ], big + 38912)
        mk = at("mk", [HP, SEQ], big + 47104)
        mv = at("mv", [QT, SEQ], big + 55296)
        mvT = at("mvT", [HP, SEQ], big + 63488)
        lat_sq = at("lat_sq", [3, SEQ], big + 63488)
        relu = at("relu", [3, SEQ], big + 63488)
        prob = at("prob", [3, SEQ], big + 63488)
        probT = at("probT", [2, SEQ], big + 69632)
        kw = at("kw", [QT, 68], big + 71680)
        max8 = at("max8", [3, 8], big + 73728)
        gate = at("gate", [2 * KD, SEQ], big + 75776)
        cq = at("cq", [2, SEQ], big + 75776)
        ckv = at("ckv", [SEQ], big + 79872)
        kiw = at("kiw", [SEQ], big + 81920)
        s_uq = at("s_uq", [2, SEQ], big + 83968)
        s_qidx = at("s_qidx", [2, 256], big + 88064)
        s_uk = at("s_uk", [SEQ], big + 90112)
        s_uv = at("s_uv", [SEQ], big + 92160)
        lat_r = at("lat_r", [2, SEQ], big + 108544)
        kn = at("kn", [QT, P], big + 112640)
        y_hi = at("y_hi", [KD, SEQ], big + 38912, F32R)
        y_lo = at("y_lo", [KD, SEQ], big + 55296, F32R)
        mrg = at("mrg", [2, 3, SEQ], big)
        out_tok = at("out_tok", [QT, D_MODEL], big)
        fin = at("fin", [2, SEQ], big + 16384)
        msc = big + 114688
        ident = at("ident", [P], msc)
        ones = at("ones", [P], msc + 512)
        cols = at("cols", [P], msc + 1024)
        rows = at("rows", [P], big + 81920)
        ada_acc = at("ada_acc", [2, P], msc + 1536)
        mods = at("mods", [N_MOD * KD], msc + 2560)
        c_act = at("c_act", [KD], msc + 2880)
        a_mul = at("a_mul", [3, KD], msc + 2944)
        o_mul = at("o_mul", [3, KD], msc + 3072)
        stats = at("stats", [QT, 6], msc + 3200)
        mean = at("mean", [QT, 2], msc + 3328)
        k_rstd = at("k_rstd", [QT, 2], msc + 3392)
        widx = at("widx", [QT, IDX_HEADS], msc + 3456)
        nmax = at("nmax", [4, 1], msc + 3520)
        psumq = at("psumq", [4, 1], msc + 3552)
        rsum = at("rsum", [4, 1], msc + 3584)

        ps = ctx.enter_context(nc.psum_tensor("ps", [P, 8, SEQ], F32))
        B_SUM, B_MOD = 4, 5

        def sem(name):
            return ctx.enter_context(nc.semaphore(name))

        s_in = sem("s_in")
        s_rows = sem("s_rows")
        raw_in = [sem(f"raw_in{r}") for r in range(RAW)]
        hi_done = sem("hi_done")
        lo_done = sem("lo_done")
        unit_done = sem("unit_done")
        silu_done = sem("silu_done")
        g_done = sem("g_done")
        ghi_done = sem("ghi_done")
        glo_done = sem("glo_done")
        x_done = sem("x_done")
        sq_sem = sem("sq_sem")
        sum_done = sem("sum_done")
        ms_done = sem("ms_done")
        sqrt_done = sem("sqrt_done")
        rstd_done = sem("rstd_done")
        t_done = sem("t_done")
        h32_done = sem("h32_done")
        hhi_done = sem("hhi_done")
        hlo_done = sem("hlo_done")
        ada0_in = [sem(f"ada0_in{r}") for r in range(4)]
        ada_in = [sem(f"ada_in{r}") for r in range(4)]
        ada_step = sem("ada_step")
        ada_sum = sem("ada_sum")
        ada_used = sem("ada_used")
        ada0_dve = sem("ada0_dve")
        ada0_pool = sem("ada0_pool")
        ada0_sum = sem("ada0_sum")
        dve_ada = sem("dve_ada")
        const_done = sem("const_done")
        const_step = sem("const_step")
        ada0_step = sem("ada0_step")
        cols_psum = sem("cols_psum")
        cols_done = sem("cols_done")
        cact_done = sem("cact_done")
        xt_psum = sem("xt_psum")
        mod_done = sem("mod_done")
        mods_all = sem("mods_all")
        evac = sem("evac")
        small_in = sem("small_in")
        lsq_done = sem("lsq_done")
        lat_psum = sem("lat_psum")
        lat_dve = sem("lat_dve")
        lat_act = sem("lat_act")
        kn_psum = sem("kn_psum")
        prj_psum = sem("prj_psum")
        prj_free = sem("prj_free")
        is_psum = sem("is_psum")
        is_relu = sem("is_relu")
        is_acc = sem("is_acc")
        vt_psum = sem("vt_psum")
        vt_done = sem("vt_done")
        causal_done = sem("causal_done")
        dist_done = sem("dist_done")
        tk_step = sem("tk_step")
        s_psum = sem("s_psum")
        s_used = sem("s_used")
        m_done = sem("m_done")
        e_done = sem("e_done")
        r_done = sem("r_done")
        p_done = sem("p_done")
        pt_psum = sem("pt_psum")
        pt_done = sem("pt_done")
        pv_done = sem("pv_done")
        ohi_done = sem("ohi_done")
        olo_done = sem("olo_done")
        mg_step = sem("mg_step")
        mg_free = sem("mg_free")
        mg_y = sem("mg_y")
        yhi_done = sem("yhi_done")
        ylo_done = sem("ylo_done")
        fin_done = sem("fin_done")
        fin_psum = sem("fin_psum")
        fin_act = sem("fin_act")
        fin_dve = sem("fin_dve")
        s_out = sem("s_out")

        def ktiles(w):
            return w.rearrange("(k p) n -> p k n", p=P)

        w_up = [[ktiles(w1_ffn1[0]), ktiles(w3_ffn1[0])], [ktiles(w1_ffn2[0]), ktiles(w3_ffn2[0])]]
        w_dn = [ktiles(w2_ffn1[0]), ktiles(w2_ffn2[0])]
        w_in_v, w_out_v = ktiles(w_in[0]), ktiles(w_out[0])
        w_pd_v, w_pm_v = ktiles(w_proj_dsa[0]), ktiles(w_proj_moba[0])
        w_ada_v = ktiles(w_ada[0])

        def nk_of(u):
            return KH if U_DOWN[0] <= u < U_LAT or u >= U_DOWN[1] else KD

        N_UNITS = U_DOWN[1] + 2 * KD

        def done(u):
            return u + 1 + SPL

        def split(u):
            return u + 1 + RAW

        def load_unit(sp, u, j, first, second, nk):
            sp.wait_ge(lo_done, u + 1)
            dst = raw[j][:, 0:nk * P].rearrange("p (k n) -> p k n", k=nk)
            m = first.shape[1]
            sp.dma_start(dst[:, 0:m], first).then_inc(raw_in[j], 16)
            sp.dma_start(dst[:, m:nk], second).then_inc(raw_in[j], 16)

        def load_cols(sp, u, j, w, col, k0, nk):
            m = nk // 2
            load_unit(sp, u, j, w[:, k0:k0 + m, bass.ds(col, P)], w[:, k0 + m:k0 + nk, bass.ds(col, P)], nk)

        def arrivals(u4):
            return 32 * (u4 + 1)

        def split_hi(act, u4, j, nk):
            act.wait_ge(raw_in[j], arrivals(u4))
            act.wait_ge(unit_done, 4 * u4 + j + 1)
            nc.scalar.activation(w_hi[j % SPL][:, 0:nk * P], raw[j][:, 0:nk * P], ACT.Copy).then_inc(hi_done, 1)

        def split_lo(dve, u4, j, nk):
            dve.wait_ge(hi_done, 4 * u4 + j + 1)
            nc.vector.tensor_tensor(w_lo[j % SPL][:, 0:nk * P], raw[j][:, 0:nk * P],
                                    w_hi[j % SPL][:, 0:nk * P].bitcast(F32), ALU.subtract).then_inc(lo_done, 1)

        def hi_u(act, u):
            if u < N_UNITS:
                split_hi(act, u // 4, u % 4, nk_of(u))

        def lo_u(dve, u):
            if u < N_UNITS:
                split_lo(dve, u // 4, u % 4, nk_of(u))

        def mm3(bank, j, kk, rhs_hi, rhs_lo, start, stop):
            hi = w_hi[j % SPL][:, kk * P:(kk + 1) * P]
            lo = w_lo[j % SPL][:, kk * P:(kk + 1) * P]
            nc.tensor.matmul(ps[:, bank, :], hi, rhs_hi, start=start, stop=False)
            nc.tensor.matmul(ps[:, bank, :], hi, rhs_lo, start=False, stop=False)
            return nc.tensor.matmul(ps[:, bank, :], lo, rhs_hi, start=False, stop=stop)

        def unit(bank, j, rhs_hi, rhs_lo, nk=KD, k0=0, start=True, stop=True):
            for kk in range(nk):
                last = mm3(bank, j, kk, rhs_hi[:, k0 + kk, :], rhs_lo[:, k0 + kk, :],
                           start and kk == 0, stop and kk == nk - 1)
            return last

        def pool_square(pool, n, k):
            pool.wait_ge(x_done, KD * n + k + 1)
            if k == 0:
                if n:
                    pool.wait_ge(sum_done, n)
                nc.gpsimd.tensor_tensor(tmp[:, 2, :], xT[:, 0, :], xT[:, 0, :], ALU.mult).then_inc(sq_sem, 1)
                return
            c = (2 * KD - 1) * n + 2 * k - 1
            nc.gpsimd.tensor_tensor(tmp[:, 0, :], xT[:, k, :], xT[:, k, :], ALU.mult).then_inc(sq_sem, 1)
            pool.wait_ge(sq_sem, c + 1)
            nc.gpsimd.tensor_tensor(tmp[:, 2, :], tmp[:, 2, :], tmp[:, 0, :], ALU.add).then_inc(sq_sem, 1)
            if k < KD - 1:
                pool.wait_ge(sq_sem, c + 2)

        def pe_sum(pe, n):
            pe.wait_ge(sq_sem, (2 * KD - 1) * (n + 1))
            nc.tensor.matmul(ps[:, B_SUM, :], ones[:, :], tmp[:, 2, :], start=True, stop=True).then_inc(sum_done, 1)

        def dve_rstd(dve, n):
            dve.wait_ge(sum_done, n + 1)
            nc.vector.tensor_scalar(tmp[:, 3, :], ps[:, B_SUM, :], 1.0 / D_MODEL, EPS, ALU.mult,
                                    ALU.add).then_inc(ms_done, 1)
            dve.wait_ge(sqrt_done, n + 1)
            nc.vector.reciprocal(tmp[:, 3, :], tmp[:, 3, :]).then_inc(rstd_done, 1)
            dve.wait_ge(rstd_done, n + 1)

        def act_sqrt(act, n):
            act.wait_ge(ms_done, n + 1)
            nc.scalar.activation(tmp[:, 3, :], tmp[:, 3, :], ACT.Sqrt).then_inc(sqrt_done, 1)

        def dve_h(dve, n):
            dve_rstd(dve, n)

            def low(k):
                dve.wait_ge(h32_done, KD * n + k + 1)
                dve.wait_ge(hhi_done, KD * n + k + 1)
                nc.vector.tensor_tensor(h_lo[:, k, :], nrm[:, 2 + k % 2, :], h_hi[:, k, :].bitcast(F32),
                                        ALU.subtract).then_inc(hlo_done, 1)

            for k in range(KD):
                if k >= 2:
                    dve.wait_ge(hhi_done, KD * n + k - 1)
                nc.vector.tensor_tensor(nrm[:, k % 2, :], xT[:, k, :], tmp[:, 3, :], ALU.mult).then_inc(t_done, 1)
                if k:
                    low(k - 1)
                dve.wait_ge(t_done, KD * n + k + 1)
                nc.vector.tensor_scalar(nrm[:, 2 + k % 2, :], nrm[:, k % 2, :], a_mul[:, n, k:k + 1],
                                        mods[:, 24 * n + k:24 * n + k + 1], ALU.mult, ALU.add).then_inc(h32_done, 1)
            low(KD - 1)

        def act_h(act, n):
            act_sqrt(act, n)
            for k in range(KD):
                act.wait_ge(t_done, KD * n + k + 1)
                nc.scalar.activation(h_hi[:, k, :], nrm[:, k % 2, :], ACT.Identity, bias=mods[:, 24 * n + k:24 * n + k + 1],
                                     scale=a_mul[:, n, k:k + 1]).then_inc(hhi_done, 1)

        def sp_ffn(sp, f):
            with sp.Fori(0, KF // 2) as i:
                for j in range(4):
                    load_cols(sp, U_UP[f] + 4 * i + j, j, w_up[f][j % 2], i * (2 * P) + (j // 2) * P, 0, KD)
            with sp.Fori(0, KD // 2) as i:
                for j in range(4):
                    load_cols(sp, U_DOWN[f] + 4 * i + j, j, w_dn[f], i * (2 * P) + (j // 2) * P, (j % 2) * KH, KH)

        def pe_ada(pe, n, slot):
            pe.wait_ge(ada_sum, n + 1)
            nc.tensor.matmul(ps[:, B_MOD, bass.ds(n + ADA_FIRST, 1)], ada_acc[:, slot, :], ones[:, 0:1],
                             start=True, stop=True).then_inc(ada_used, 1)

        def pe_ffn(pe, f):
            with pe.Fori(0, KF // 2) as i:
                for j in range(4):
                    pe.wait_ge(lo_done, U_UP[f] + 4 * i + j + 1 + RAW)
                    if j % 2 == 0:
                        pe.wait_ge(g_done, KF * f + 2 * i + j // 2 + 1)
                    for kk in range(KD):
                        if j == 0:
                            pe.wait_ge(hlo_done, KD * 2 * f + kk + 1)
                        last = mm3(j, j, kk, h_hi[:, kk, :], h_lo[:, kk, :], kk == 0, kk == KD - 1)
                    last.then_inc(unit_done, 1)
                    if f == 0:
                        pe_ada(pe, 4 * i + j, j % 2)
            with pe.Fori(0, KD // 2) as i:
                for j in range(4):
                    pe.wait_ge(lo_done, U_DOWN[f] + 4 * i + j + 1 + RAW)
                    if j % 2 == 0:
                        pe.wait_ge(g_done, KF * (f + 1) + 1)
                        pe.wait_ge(x_done, KD * (1 + 2 * f) + 2 * i + j // 2 - 1)
                    pe.wait_ge(glo_done, KF * f + KH * (j % 2 + 1))
                    last = unit(j // 2, j, g_hi, g_lo, nk=KH, k0=KH * (j % 2), start=j % 2 == 0, stop=j % 2 == 1)
                    last.then_inc(unit_done, 1)
                    if f == 0 and j < 2:
                        pe.wait_ge(mod_done, 4)
                        pe_ada(pe, 2 * KF + 2 * i + j, j)

        def act_pair(act, f, i, jp, nk):
            u = U_UP[f] + 4 * i + 2 * jp
            pair = KF * f + 2 * i + jp
            split_hi(act, U_UP[f] // 4 + i + (jp == 1), (2 * jp + 2) % 4, nk)
            act.wait_ge(unit_done, u + 1 + SPL)
            act.wait_ge(g_done, pair + 1)
            nc.scalar.activation(tmp[:, jp, :], ps[:, 2 * jp, :], ACT.Silu).then_inc(silu_done, 1)
            split_hi(act, U_UP[f] // 4 + i + (jp == 1), (2 * jp + 3) % 4, nk)
            act.wait_ge(g_done, pair + 1 + 2)
            nc.scalar.activation(g_hi[:, bass.ds(2 * i + jp, 1), :], tmp[:, 2 + jp:3 + jp, :],
                                 ACT.Copy).then_inc(ghi_done, 1)
            if f == 0:
                for j in (2 * jp, 2 * jp + 1):
                    act_ada(act, 4 * i + j + 4, j)

        def act_ada(act, n, slot):
            act.wait_ge(ada_sum, n - 3)
            act.dma_start(ada[:, slot], w_ada_v[:, :, bass.ds(n * P + ADA_FIRST * P, P)]).then_inc(ada_in[slot], 16)

        def dve_pair(dve, f, i, jp, nk):
            pair = KF * f + 2 * i + jp
            for q in (2, 3):
                split_lo(dve, U_UP[f] // 4 + i + (jp == 1), (2 * jp + q) % 4, nk)
            dve.wait_ge(silu_done, pair + 1)
            dve.wait_ge(unit_done, U_UP[f] + 4 * i + 2 * jp + 2 + SPL)
            nc.vector.tensor_tensor(tmp[:, 2 + jp, :], tmp[:, jp, :], ps[:, 2 * jp + 1, :],
                                    ALU.mult).then_inc(g_done, 1)
            dve.wait_ge(ghi_done, pair + 1)
            nc.vector.tensor_tensor(g_lo[:, bass.ds(2 * i + jp, 1), :], tmp[:, 2 + jp:3 + jp, :],
                                    g_hi[:, bass.ds(2 * i + jp, 1), :].bitcast(F32), ALU.subtract).then_inc(glo_done, 1)

        def pairs(eng, f, step):
            with eng.Fori(0, KF // 2 - 1) as i:
                step(eng, f, i, 0, KD)
                step(eng, f, i, 1, KD)
            step(eng, f, KF // 2 - 1, 0, KD)
            step(eng, f, KF // 2 - 1, 1, KH)

        def act_down(act, f):
            for d in range(KD):
                hi_u(act, U_DOWN[f] + 2 * d + 2)
                hi_u(act, U_DOWN[f] + 2 * d + 3)
                if f == 0 and d < 4:
                    act_ada(act, 2 * KF + 4 + d, d)

        def residual(dve, n, d, bank):
            nc.vector.scalar_tensor_tensor(xT[:, d, :], ps[:, bank, :], o_mul[:, n, d:d + 1], xT[:, d, :],
                                           ALU.mult, ALU.add).then_inc(x_done, 1)

        def dve_down(dve, f):
            if f == 0:
                dve_gate(dve)
            for d in range(KD):
                lo_u(dve, U_DOWN[f] + 2 * d + 2)
                lo_u(dve, U_DOWN[f] + 2 * d + 3)
                dve.wait_ge(unit_done, done(U_DOWN[f] + 2 * d + 1))
                residual(dve, 2 * f, d, d % 2)

        def dve_gate(dve):
            dve.wait_ge(ada_used, 2 + 2 * KF)
            nc.vector.tensor_tensor(mods[:, 16:24], ps[:, B_MOD, 16:24], cols[:, 16:24], ALU.add).then_inc(mod_done, 1)
            dve.wait_ge(mod_done, 3)
            nc.vector.tensor_scalar(o_mul[:, 0, :], mods[:, 16:24], 0.5, 0.5, ALU.mult, ALU.add).then_inc(mod_done, 1)
            dve.wait_ge(mod_done, 4)

        def dve_mods(dve):
            dve.wait_ge(ada_used, 2 + N_MOD * KD - ADA_FIRST)
            nc.vector.tensor_tensor(mods[:, 24:72], ps[:, B_MOD, 24:72], cols[:, 24:72], ALU.add).then_inc(mod_done, 1)
            dve.wait_ge(mod_done, 5)
            nc.vector.tensor_scalar(o_mul[:, 1, :], mods[:, 40:48], 1.0, None, ALU.add).then_inc(mod_done, 1)
            nc.vector.tensor_scalar(o_mul[:, 2, :], mods[:, 64:72], 0.5, 0.5, ALU.mult, ALU.add).then_inc(mod_done, 1)
            for n, r in ((1, R_GM), (2, R_G2)):
                nc.vector.scalar_tensor_tensor(a_mul[:, n, :], mods[:, 24 * n + 8:24 * n + 16], 1.0, cols[:, r:r + KD],
                                               ALU.add, ALU.mult).then_inc(mod_done, 1)
            dve.wait_ge(mod_done, 9)

        steps = [(b, hp, e, c) for b in range(2) for hp in range(HP) for e in range(2) for c in range(QT)]
        NST = len(steps)
        B_S, B_T, B_O = (0, 1), (2, 3), (6, 7)

        block = ctx.enter_context(nc.Block())

        @block.sync
        def _(sp):
            for r, src in ((R_BADA, b_ada), (R_G1, g_ffn1), (R_GM, g_mix), (R_G2, g_ffn2), (R_CQ, g_cq), (R_CKV, g_ckv),
                           (R_C, c_in)):
                v = src[0].rearrange("(r n) -> r n", n=P)
                sp.dma_start(rows[r:r + v.shape[0], :], v).then_inc(s_rows, 16)
            sp.dma_start(rows[R_GF:R_GF + KD, :], g_final.rearrange("(r n) -> r n", n=P)).then_inc(s_rows, 16)
            for r, src in ((R_GK, g_kidx), (R_BK, b_kidx)):
                for half in range(2):
                    sp.dma_start(rows[r:r + 1, 64 * half:64 * half + 64], src).then_inc(s_rows, 16)
            for t in range(QT):
                sp.dma_start(x_tok[:, t, :], x_in[0, t * P:(t + 1) * P, :]).then_inc(s_in, 16)
            for r in range(4):
                for t in range(5 * r, 5 * r + 5):
                    sp.dma_start(ada0[:, t], w_ada_v[:, :, t * P:(t + 1) * P]).then_inc(ada0_in[r], 16)
            sp_ffn(sp, 0)
            for q in range(4):
                load_cols(sp, U_LAT + q, q, w_in_v, q * P, 0, KD)
            for q in range(4):
                load_cols(sp, U_QKV + q, q, w_in_v, QKV_COL + q * P, 0, KD)
            sp.wait_ge(unit_done, done(U_LAT - 1))
            sp.dma_start(s_uq[:], w_uq[0].rearrange("(k p) h d -> p k (h d)", p=P)).then_inc(small_in, 16)
            sp.dma_start(s_qidx[:], w_qidx[0].rearrange("(k p) h d -> p k (h d)", p=P)).then_inc(small_in, 16)
            sp.dma_start(s_uk[:], w_uk[0].rearrange("p h d -> p (h d)")).then_inc(small_in, 16)
            sp.dma_start(s_uv[:], w_uv[0].rearrange("p h d -> p (h d)")).then_inc(small_in, 16)
            with sp.Fori(0, 6) as i:
                for j in range(4):
                    load_cols(sp, U_QKV + 4 + 4 * i + j, j, w_in_v, i * (4 * P) + (QKV_COL + (4 + j) * P), 0, KD)
            for q in range(KD):
                load_unit(sp, U_MERGE + q, q % 4, w_pd_v[:, :, q * P:(q + 1) * P], w_pm_v[:, :, q * P:(q + 1) * P], KD)
            for q in range(KD):
                load_cols(sp, U_OUT + q, q % 4, w_out_v, q * P, 0, KD)
            sp_ffn(sp, 1)
            for half in range(2):
                for t in range(QT):
                    sp.wait_ge(fin_act if t % 2 == 0 else fin_dve, 2 * half + t // 2 + 1)
                    sp.dma_start(out[0, t * P:(t + 1) * P, half * 512:half * 512 + 512],
                                 out_tok[:, t, half * 512:half * 512 + 512]).then_inc(s_out, 16)
            sp.wait_ge(s_out, 16 * 2 * QT)

        @block.tensor
        def _(pe):
            pe.sem_inc(unit_done, SPL)
            pe.sem_inc(ada_used, 2)
            pe.wait_ge(s_rows, 16 * 12)
            pe.wait_ge(const_done, 2)
            nc.tensor.transpose(ps[:, B_MOD, 0:N_ROWS], rows[0:N_ROWS, :], ident[0:N_ROWS, 0:N_ROWS]).then_inc(cols_psum, 1)
            pe.wait_ge(s_in, 16 * QT)
            for k in range(KD):
                bank = (0, 1, 2, 3)[k % 4]
                if k >= 4:
                    pe.wait_ge(x_done, k - 3)
                for t in range(QT):
                    last = nc.tensor.transpose(ps[:, bank, t * P:(t + 1) * P], x_tok[:, t, k * P:(k + 1) * P], ident[:, :])
                last.then_inc(xt_psum, 1)
            pe.wait_ge(cols_done, 1)
            for n in range(ADA_FIRST):
                if n < ADA_DVE:
                    pe.wait_ge(ada0_dve, n + 1)
                else:
                    pe.wait_ge(ada0_pool, n + 1 - ADA_DVE)
                last = nc.tensor.matmul(ps[:, B_MOD, n:n + 1], ada0[:, n, 0, :], ones[:, 0:1], start=True, stop=True)
                if n == 15:
                    last.then_inc(ada0_sum, 1)
                    pe_sum(pe, 0)
                    pe.wait_ge(mod_done, 1)
            pe_ffn(pe, 0)
            pe_sum(pe, 1)

            def single(u, first=False):
                pe.wait_ge(lo_done, split(u))
                if u >= U_LAT + 4:
                    pe.wait_ge(evac, u - U_LAT - 3)
                for kk in range(KD):
                    if first:
                        pe.wait_ge(hlo_done, KD + kk + 1)
                    last = mm3(u % 4, u, kk, h_hi[:, kk, :], h_lo[:, kk, :], kk == 0, kk == KD - 1)
                last.then_inc(unit_done, 1)

            for q in range(4):
                single(U_LAT + q, q == 0)
            single(U_QKV)
            single(U_QKV + 1)
            pe.wait_ge(lsq_done, 3)
            nc.tensor.matmul(ps[:, 4, :], ones[:, :], lat_sq[:, 0, :], start=True, stop=False)
            nc.tensor.matmul(ps[:, 4, :], ones[:, :], lat_sq[:, 1, :], start=False, stop=True).then_inc(lat_psum, 1)
            nc.tensor.matmul(ps[:, 6, :], ones[:, :], lat_sq[:, 2, :], start=True, stop=True).then_inc(lat_psum, 1)
            pe.wait_ge(evac, 4)
            for t in range(QT):
                last = nc.tensor.transpose(ps[:, 7, t * 68:(t + 1) * 68], kiw[0:68, t * P:(t + 1) * P], ident[0:68, 0:68])
            last.then_inc(lat_psum, 1)
            for q in range(2, 6):
                single(U_QKV + q)
            pe.wait_ge(lat_dve, 17)
            for t in range(QT):
                last = nc.tensor.transpose(ps[:, 7, t * P:(t + 1) * P], kn[:, t, :], ident[:, :])
            last.then_inc(kn_psum, 1)
            pe.wait_ge(small_in, 64)
            for n in range(14):
                bank = 4 + n % 3
                if n >= 3:
                    pe.wait_ge(prj_free, n - 2)
                if n < 6:
                    for r in range(2):
                        w = s_qidx[:, r, n * P:(n + 1) * P] if n < 2 else s_uq[:, r, (n - 2) * P:(n - 1) * P]
                        last = nc.tensor.matmul(ps[:, bank, :], w, cq[:, r, :], start=r == 0, stop=r == 1)
                elif n < 10:
                    last = nc.tensor.matmul(ps[:, bank, :], s_uk[:, (n - 6) * P:(n - 5) * P], ckv[:, :], start=True, stop=True)
                else:
                    last = nc.tensor.matmul(ps[:, bank, :], ckv[:, (n - 10) * P:(n - 9) * P], s_uv[:, :], start=True, stop=True)
                last.then_inc(prj_psum, 1)
            for q in range(6, 12):
                single(U_QKV + q)
            pe.wait_ge(evac, 16)
            for t in range(QT):
                bank = (7, 4, 5, 6)[t]
                if t == 0:
                    pe.wait_ge(lat_dve, 18)
                if t == 1:
                    pe.wait_ge(prj_free, 14)
                for hp in range(HP):
                    last = nc.tensor.transpose(ps[:, bank, hp * P:(hp + 1) * P], mvT[:, hp, t * P:(t + 1) * P], ident[:, :])
                last.then_inc(vt_psum, 1)
            pe.wait_ge(vt_done, 4)
            n = 0
            for c in range(1, QT):
                for h in range(IDX_HEADS):
                    if n >= 3:
                        pe.wait_ge(is_relu, n - 2)
                    o = 64 * (h % 2)
                    nc.tensor.matmul(ps[:, 4 + n % 3, 0:(c + 1) * P], qi[o:o + 64, h // 2, c * P:(c + 1) * P],
                                     ki[o:o + 64, 0:(c + 1) * P], start=True, stop=True).then_inc(is_psum, 1)
                    n += 1
            with pe.Fori(0, 4) as i:
                for j in range(4):
                    pe.wait_ge(lo_done, U_GATE + 4 * i + j + 1 + RAW)
                    pe.wait_ge(evac, U_GATE - U_LAT - 3 + 4 * i + j)
                    unit(j, j, h_hi, h_lo).then_inc(unit_done, 1)
            pe.wait_ge(evac, 32)

            def scores(n):
                b, hp, e, c = steps[n]
                q, k = ((mq, mk), (dq, dk))[b]
                if n >= 2:
                    pe.wait_ge(s_used, n - 1)
                o = 64 * e
                nc.tensor.matmul(ps[:, B_S[n % 2], 0:(c + 1) * P], q[o:o + 64, hp, c * P:(c + 1) * P],
                                 k[o:o + 64, hp, 0:(c + 1) * P], start=True, stop=True).then_inc(s_psum, 1)

            def transposes(n):
                c = steps[n][3]
                pe.wait_ge(p_done, n + 1)
                if n >= 2:
                    pe.wait_ge(pt_done, n - 1)
                for s in range(c + 1):
                    last = nc.tensor.transpose(ps[:, B_T[n % 2], s * P:(s + 1) * P], prob[:, n % 3, s * P:(s + 1) * P], ident[:, :])
                last.then_inc(pt_psum, 1)

            def values(n):
                b, hp, e, c = steps[n]
                v = (mv, dv)[b]
                pair = HP * b + hp
                pe.wait_ge(pt_done, n + 1)
                if pair >= 2 and e == 0 and c == 0:
                    pe.wait_ge(olo_done, pair - 1)
                for s in range(c + 1):
                    last = nc.tensor.matmul(ps[64 * e:64 * e + 64, B_O[pair % 2], c * P:(c + 1) * P],
                                            v[:, s, hp * P + 64 * e:hp * P + 64 * e + 64], probT[:, n % 2, s * P:(s + 1) * P],
                                            start=s == 0, stop=s == c)
                last.then_inc(pv_done, 1)

            for n in range(NST + 3):
                if n < NST:
                    scores(n)
                if 2 <= n < NST + 2:
                    transposes(n - 2)
                if n >= 3:
                    values(n - 3)
            for q in range(KD):
                pe.wait_ge(lo_done, split(U_MERGE + q))
                if q >= 2:
                    pe.wait_ge(mg_free, 2 * (q - 1))
                for half in range(2):
                    for kk in range(HP):
                        tile = (1 - half) * HP + kk
                        pe.wait_ge(olo_done, 2 * HP if half == 0 else HP)
                        last = mm3(2 * (q % 2) + half, q, half * HP + kk, h_hi[:, tile, :], h_lo[:, tile, :], kk == 0, kk == HP - 1)
                last.then_inc(unit_done, 1)
            for q in range(KD):
                u = U_OUT + q
                pe.wait_ge(lo_done, split(u))
                if q < 4:
                    pe.wait_ge(mg_free, 2 * KD if q >= 2 else 2 * KD - 2)
                else:
                    pe.wait_ge(x_done, 2 * KD + q - 3)
                for kk in range(KD):
                    if q == 0:
                        pe.wait_ge(ylo_done, kk + 1)
                    last = mm3(q % 4, u, kk, y_hi[:, kk, :], y_lo[:, kk, :], kk == 0, kk == KD - 1)
                last.then_inc(unit_done, 1)
            pe_sum(pe, 2)
            pe_ffn(pe, 1)
            pe_sum(pe, 3)
            for k in range(KD):
                pe.wait_ge(fin_done, k + 1)
                for t in range(QT):
                    last = nc.tensor.transpose(ps[:, 4 * (k // 4) + t, (k % 4) * P:(k % 4 + 1) * P],
                                               fin[:, k % 2, t * P:(t + 1) * P], ident[:, :])
                last.then_inc(fin_psum, 1)

        @block.scalar
        def _(act):
            act.wait_ge(cols_done, 1)
            nc.scalar.activation(c_act[:, :], cols[:, R_C:R_C + KD], ACT.Silu).then_inc(cact_done, 1)
            act.wait_ge(xt_psum, KD)
            for n in range(4):
                act.dma_start(ada[:, n], w_ada_v[:, :, (ADA_FIRST + n) * P:(ADA_FIRST + n + 1) * P]).then_inc(ada_in[n], 16)
            hi_u(act, 0)
            hi_u(act, 1)
            act_h(act, 0)
            pairs(act, 0, act_pair)
            act_down(act, 0)
            act_h(act, 1)

            def copy_out(u, dst, func=ACT.Copy, scale=1.0):
                act.wait_ge(unit_done, done(u))
                nc.scalar.activation(dst, ps[:, u % 4, :], func, scale=scale).then_inc(evac, 1)

            lat = [cq[:, 0, :], cq[:, 1, :], ckv[:, :], kiw[:, :]]
            for q in range(16):
                u = U_LAT + q
                hi_u(act, u + 2)
                if q < 4:
                    copy_out(u, lat[q])
                else:
                    hp = (q - 4) % HP
                    dst = (mq, mk, mvT)[(q - 4) // HP]
                    if q == 12:
                        act.wait_ge(lat_psum, 3)
                    copy_out(u, dst[:, hp, :], scale=HEAD_DIM ** -0.5 if q < 8 else 1.0)
                if q == 6:
                    for n, (buf, cnt) in enumerate(((lat_r[:, 0, :], 1), (lat_r[:, 1, :], 2), (k_rstd[:, :, 0], 12))):
                        act.wait_ge(lat_dve, cnt)
                        nc.scalar.activation(buf, buf, ACT.Sqrt).then_inc(lat_act, 1)
            n = 0
            for c in range(1, QT):
                for h in range(IDX_HEADS):
                    act.wait_ge(is_psum, n + 1)
                    if n >= 3:
                        act.wait_ge(is_acc, n - 2)
                    else:
                        act.wait_ge(vt_psum, 4)
                    nc.scalar.activation(relu[:, n % 3, 0:(c + 1) * P], ps[:, 4 + n % 3, 0:(c + 1) * P], ACT.Relu,
                                         scale=(IDX_HEADS * 64) ** -0.5).then_inc(is_relu, 1)
                    n += 1
            with act.Fori(0, 3) as i:
                for j in range(4):
                    split_hi(act, U_GATE // 4 + i + (j >= 2), (j + 2) % 4, KD)
                    act.wait_ge(unit_done, U_GATE + 4 * i + j + 1 + SPL)
                    nc.scalar.activation(gate[:, bass.ds(4 * i + j, 1), :], ps[:, j:j + 1, :], ACT.Sigmoid).then_inc(evac, 1)
            for q in range(12, 16):
                hi_u(act, U_GATE + q + 2)
                act.wait_ge(unit_done, done(U_GATE + q))
                nc.scalar.activation(gate[:, q, :], ps[:, q % 4, :], ACT.Sigmoid).then_inc(evac, 1)

            def exps(n):
                c = steps[n][3]
                act.wait_ge(m_done, n + 1)
                nc.scalar.activation(prob[:, n % 3, 0:(c + 1) * P], prob[:, n % 3, 0:(c + 1) * P], ACT.Exp,
                                     bias=nmax[:, n % 4, :], accum_out=psumq[:, n % 4, :]).then_inc(e_done, 1)

            def copies(n):
                c = steps[n][3]
                act.wait_ge(pt_psum, n + 1)
                if n >= 2:
                    act.wait_ge(pv_done, n - 1)
                nc.scalar.activation(probT[:, n % 2, 0:(c + 1) * P], ps[:, B_T[n % 2], 0:(c + 1) * P], ACT.Copy)\
                    .then_inc(pt_done, 1)

            def o_high(pair):
                act.wait_ge(pv_done, 8 * (pair + 1))
                nc.scalar.activation(h_hi[:, pair, :], ps[:, B_O[pair % 2], :], ACT.Copy).then_inc(ohi_done, 1)

            for n in range(NST + 4):
                if n < NST:
                    exps(n)
                if 2 <= n < NST + 2:
                    copies(n - 2)
                if n >= 11 and (n - 11) % 8 == 0:
                    o_high((n - 11) // 8)
            for q in range(KD):
                hi_u(act, U_MERGE + q + 2)
                act.wait_ge(mg_y, q + 1)
                nc.scalar.activation(y_hi[:, q, :], mrg[:, q % 2, 2, :], ACT.Copy).then_inc(yhi_done, 1)
            for q in range(KD):
                hi_u(act, U_OUT + q + 2)
            act_h(act, 2)
            pairs(act, 1, act_pair)
            act_down(act, 1)
            act_sqrt(act, 3)
            for half in range(2):
                for t in (0, 2):
                    act.wait_ge(fin_psum, 4 * half + 4)
                    nc.scalar.activation(out_tok[:, t, half * 512:half * 512 + 512], ps[:, 4 * half + t, :],
                                         ACT.Copy).then_inc(fin_act, 1)

        @block.vector
        def _(dve):
            dve.sem_inc(lo_done, RAW)
            dve.sem_inc(g_done, 2)
            dve.sem_inc(tk_step, 3)
            nc.vector.memset(ones[:, :], 1.0).then_inc(const_done, 1)
            dve.wait_ge(cols_psum, 1)
            nc.vector.tensor_copy(cols[:, 0:N_ROWS], ps[:, B_MOD, 0:N_ROWS]).then_inc(cols_done, 1)
            for k in range(KD):
                dve.wait_ge(xt_psum, k + 1)
                nc.vector.tensor_copy(xT[:, k, :], ps[:, k % 4, :]).then_inc(x_done, 1)
            dve.wait_ge(cact_done, 1)
            n = 0
            for t in range(ADA_DVE):
                dve.wait_ge(ada0_in[t // 5], 80)
                a = ada0[:, t]
                nc.vector.tensor_tensor(a, a, c_act[:, :].unsqueeze(2).broadcast_to([P, KD, P]), ALU.mult).then_inc(dve_ada, 1)
                for m in (4, 2, 1):
                    n += 1
                    dve.wait_ge(dve_ada, n)
                    last = nc.vector.tensor_tensor(a[:, 0:m, :], a[:, 0:m, :], a[:, m:2 * m, :], ALU.add)
                    last.then_inc(ada0_dve if m == 1 else dve_ada, 1)
            dve.wait_ge(ada0_sum, 1)
            nc.vector.tensor_tensor(mods[:, 0:16], ps[:, B_MOD, 0:16], cols[:, 0:16], ALU.add).then_inc(mod_done, 1)
            dve.wait_ge(mod_done, 1)
            nc.vector.scalar_tensor_tensor(a_mul[:, 0, :], mods[:, 8:16], 1.0, cols[:, R_G1:R_G1 + KD],
                                           ALU.add, ALU.mult).then_inc(mod_done, 1)
            dve.wait_ge(mod_done, 2)
            lo_u(dve, 0)
            lo_u(dve, 1)
            dve_h(dve, 0)
            pairs(dve, 0, dve_pair)
            dve_down(dve, 0)
            dve_mods(dve)
            dve_h(dve, 1)

            for q in range(4):
                lo_u(dve, U_LAT + q + 2)
            lo_u(dve, U_QKV + 2)
            lo_u(dve, U_QKV + 3)
            dve.wait_ge(lat_psum, 1)
            nc.vector.tensor_scalar(lat_r[:, 0, :], ps[:, 4, :], 1.0 / 256, EPS, ALU.mult, ALU.add).then_inc(lat_dve, 1)
            dve.wait_ge(lat_psum, 2)
            nc.vector.tensor_scalar(lat_r[:, 1, :], ps[:, 6, :], 1.0 / 128, EPS, ALU.mult, ALU.add).then_inc(lat_dve, 1)
            dve.wait_ge(lat_psum, 3)
            nc.vector.tensor_copy(kw[:, :, :], ps[:, 7, 0:QT * 68].rearrange("p (t n) -> p t n", t=QT)).then_inc(lat_dve, 1)
            dve.wait_ge(lat_dve, 3)
            for t in range(QT):
                nc.vector.bn_stats(stats[:, t, :], kw[:, t, 0:64]).then_inc(lat_dve, 1)
            for t in range(QT):
                dve.wait_ge(lat_dve, 4 + t)
                nc.vector.bn_aggr(mean[:, t, :], stats[:, t, :]).then_inc(lat_dve, 1)
            dve.wait_ge(lat_dve, 11)
            nc.vector.tensor_scalar(k_rstd[:, :, 0], mean[:, :, 1], EPS, None, ALU.add).then_inc(lat_dve, 1)
            lo_u(dve, U_QKV + 4)
            dve.wait_ge(lat_act, 3)
            nc.vector.reciprocal(k_rstd[:, :, 1], k_rstd[:, :, 0]).then_inc(lat_dve, 1)
            dve.wait_ge(lat_dve, 13)
            for t in range(QT):
                for half in range(2):
                    last = nc.vector.tensor_scalar(kn[:, t, 64 * half:64 * half + 64], kw[:, t, 0:64], mean[:, t, 0:1],
                                                   k_rstd[:, t, 1:2], ALU.subtract, ALU.mult)
            nc.vector.tensor_copy(widx[:, :, :], kw[:, :, 64:68]).then_inc(lat_dve, 1)
            for r in range(2):
                nc.vector.reciprocal(lat_r[:, r, :], lat_r[:, r, :]).then_inc(lat_dve, 1)
            lo_u(dve, U_QKV + 5)
            dve.wait_ge(lat_dve, 16)
            for r in range(2):
                nc.vector.scalar_tensor_tensor(cq[:, r, :], cq[:, r, :], cols[:, R_CQ + r:R_CQ + r + 1], lat_r[:, 0, :],
                                               ALU.mult, ALU.mult)
            nc.vector.scalar_tensor_tensor(ckv[:, :], ckv[:, :], cols[:, R_CKV:R_CKV + 1], lat_r[:, 1, :],
                                           ALU.mult, ALU.mult).then_inc(lat_dve, 1)
            lo_u(dve, U_QKV + 6)
            lo_u(dve, U_QKV + 7)
            dve.wait_ge(kn_psum, 1)
            nc.vector.tensor_scalar(ki[:, :], ps[:, 7, :], cols[:, R_GK:R_GK + 1], cols[:, R_BK:R_BK + 1],
                                    ALU.mult, ALU.add).then_inc(lat_dve, 1)
            dst = [qi[:, 0, :], qi[:, 1, :]] + [dq[:, r, :] for r in range(HP)] + [dk[:, r, :] for r in range(HP)] \
                + [dv[:, r, :] for r in range(QT)]
            for n in range(14):
                dve.wait_ge(prj_psum, n + 1)
                if 2 <= n < 6:
                    nc.vector.tensor_scalar(dst[n], ps[:, 4 + n % 3, :], HEAD_DIM ** -0.5, None, ALU.mult).then_inc(prj_free, 1)
                else:
                    nc.vector.tensor_copy(dst[n], ps[:, 4 + n % 3, :]).then_inc(prj_free, 1)
            for q in range(6, 12):
                lo_u(dve, U_QKV + q + 2)
            for t in range(QT):
                dve.wait_ge(vt_psum, t + 1)
                nc.vector.tensor_copy(mv[:, t, :], ps[:, (7, 4, 5, 6)[t], :]).then_inc(vt_done, 1)
            n = 0
            for c in range(1, QT):
                w = (c + 1) * P
                for h in range(IDX_HEADS):
                    sc = score[:, c - 1, 0:w]
                    dve.wait_ge(is_relu, n + 1)
                    if h == 0:
                        nc.vector.tensor_scalar(sc, relu[:, n % 3, 0:w], widx[:, c, 0:1], None, ALU.mult).then_inc(is_acc, 1)
                    else:
                        dve.wait_ge(is_acc, n)
                        nc.vector.scalar_tensor_tensor(sc, relu[:, n % 3, 0:w], widx[:, c, h:h + 1], sc,
                                                       ALU.mult, ALU.add).then_inc(is_acc, 1)
                    n += 1
            def select_round(done_before):
                for c in range(3):
                    dve.wait_ge(tk_step, done_before + c)
                    nc.vector.max(max8[:, c, :], score[:, c, 0:(c + 2) * P]).then_inc(tk_step, 1)
                for c in range(3):
                    dve.wait_ge(tk_step, done_before + 3 + c)
                    nc.vector.match_replace(score[:, c, 0:(c + 2) * P], max8[:, c, :], score[:, c, 0:(c + 2) * P],
                                            TAKEN).then_inc(tk_step, 1)

            dve.wait_ge(causal_done, 3)
            for q in range(16):
                lo_u(dve, U_GATE + q + 2)
                select_round(6 * q + 1)
            tk = 3 + 6 * 16
            dve.wait_ge(tk_step, tk)
            dve.wait_ge(dist_done, 2)
            for c in range(3):
                w = (c + 2) * P
                nc.vector.tensor_scalar(score[:, c, 0:w], score[:, c, 0:w], TAKEN, MASKED, ALU.not_equal, ALU.mult)\
                    .then_inc(tk_step, 1)
            for c in range(3):
                w = (c + 2) * P
                dve.wait_ge(tk_step, tk + 1 + c)
                nc.vector.tensor_tensor(score[:, c, 0:w], score[:, c, 0:w], dist[:, SEQ - w:SEQ], ALU.add).then_inc(tk_step, 1)
            dve.wait_ge(tk_step, tk + 6)

            def biased(n):
                b, hp, e, c = steps[n]
                w = (c + 1) * P
                slope = 2.0 ** (-8.0 * (2 * hp + e + 1) / HEADS)
                d = score[:, c - 1, 0:w] if b and c else dist[:, SEQ - w:SEQ]
                dve.wait_ge(s_psum, n + 1)
                if n >= 3:
                    dve.wait_ge(pt_psum, n - 2)
                nc.vector.scalar_tensor_tensor(prob[:, n % 3, 0:w], d, slope, ps[:, B_S[n % 2], 0:w],
                                               ALU.mult, ALU.add).then_inc(s_used, 1)
                dve.wait_ge(s_used, n + 1)
                nc.vector.tensor_reduce(nmax[:, n % 4, :], prob[:, n % 3, 0:w], AX.X, ALU.max, negate=True).then_inc(m_done, 1)

            def normalise(n):
                w = (steps[n][3] + 1) * P
                dve.wait_ge(e_done, n + 1)
                nc.vector.reciprocal(rsum[:, n % 4, :], psumq[:, n % 4, :]).then_inc(r_done, 1)
                dve.wait_ge(r_done, n + 1)
                nc.vector.tensor_scalar(prob[:, n % 3, 0:w], prob[:, n % 3, 0:w], rsum[:, n % 4, :], None,
                                        ALU.mult).then_inc(p_done, 1)

            def o_low(pair):
                dve.wait_ge(ohi_done, pair + 1)
                nc.vector.tensor_tensor(h_lo[:, pair, :], ps[:, B_O[pair % 2], :], h_hi[:, pair, :].bitcast(F32),
                                        ALU.subtract).then_inc(olo_done, 1)

            for n in range(NST + 4):
                if n < NST:
                    biased(n)
                if 1 <= n < NST + 1:
                    normalise(n - 1)
                if n >= 11 and (n - 11) % 8 == 0:
                    o_low((n - 11) // 8)
            for q in range(KD):
                lo_u(dve, U_MERGE + q + 2)
                dve.wait_ge(unit_done, done(U_MERGE + q))
                m = mrg[:, q % 2]
                nc.vector.tensor_tensor(m[:, 0, :], ps[:, 2 * (q % 2), :], gate[:, q, :], ALU.mult).then_inc(mg_free, 1)
                nc.vector.tensor_tensor(m[:, 1, :], ps[:, 2 * (q % 2) + 1, :], gate[:, KD + q, :], ALU.mult).then_inc(mg_free, 1)
                dve.wait_ge(mg_free, 2 * q + 2)
                nc.vector.tensor_tensor(m[:, 2, :], m[:, 0, :], m[:, 1, :], ALU.add).then_inc(mg_y, 1)
                dve.wait_ge(yhi_done, q + 1)
                nc.vector.tensor_tensor(y_lo[:, q, :], m[:, 2, :], y_hi[:, q, :].bitcast(F32), ALU.subtract).then_inc(ylo_done, 1)
            for q in range(KD):
                lo_u(dve, U_OUT + q + 2)
                dve.wait_ge(unit_done, done(U_OUT + q))
                residual(dve, 1, q, q % 4)
            dve_h(dve, 2)
            pairs(dve, 1, dve_pair)
            dve_down(dve, 1)
            dve_rstd(dve, 3)
            for k in range(KD):
                if k >= 2:
                    dve.wait_ge(fin_psum, k - 1)
                nc.vector.scalar_tensor_tensor(fin[:, k % 2, :], xT[:, k, :], cols[:, R_GF + k:R_GF + k + 1], tmp[:, 3, :],
                                               ALU.mult, ALU.mult).then_inc(fin_done, 1)
            for half in range(2):
                for t in (1, 3):
                    dve.wait_ge(fin_psum, 4 * half + 4)
                    nc.vector.tensor_copy(out_tok[:, t, half * 512:half * 512 + 512], ps[:, 4 * half + t, :]).then_inc(fin_dve, 1)

        @block.gpsimd
        def _(pool):
            nc.gpsimd.memset(ident[:, :], 1.0).then_inc(const_step, 1)
            pool.wait_ge(const_step, 1)
            nc.gpsimd.affine_select(out=ident[:, :], in_=ident[:, :], compare_op=ALU.is_equal, fill=0.0, base=0,
                                    pattern=[[-1, P]], channel_multiplier=1).then_inc(const_done, 1)
            for k in range(KD):
                pool_square(pool, 0, k)

            def column_tile(a, last_out, step, at_, wait_last=None):
                nc.gpsimd.tensor_tensor(a, a, c_act[:, :].unsqueeze(2).broadcast_to([P, KD, P]), ALU.mult)\
                    .then_inc(step, 1)
                for r, m in enumerate((4, 2)):
                    pool.wait_ge(step, at_ + r + 1)
                    nc.gpsimd.tensor_tensor(a[:, 0:m, :], a[:, 0:m, :], a[:, m:2 * m, :], ALU.add).then_inc(step, 1)
                pool.wait_ge(step, at_ + 3)
                if wait_last is not None:
                    pool.wait_ge(*wait_last)
                return nc.gpsimd.tensor_tensor(last_out, a[:, 0, :], a[:, 1, :], ALU.add)

            pool.wait_ge(cact_done, 1)
            for t in range(ADA_DVE, ADA_FIRST):
                pool.wait_ge(ada0_in[t // 5], 80)
                column_tile(ada0[:, t], ada0[:, t, 0, :], ada0_step, 3 * (t - ADA_DVE)).then_inc(ada0_pool, 1)

            def chunk(i, n, j, arrival):
                pool.wait_ge(ada_in[j], arrival)
                column_tile(ada[:, j], ada_acc[:, j % 2, :], ada_step, 3 * n, (ada_used, n + 1)).then_inc(ada_sum, 1)

            with pool.Fori(0, KF // 2) as i:
                for j in range(4):
                    chunk(i, 4 * i + j, j, 16 * i + 16)
            for d in range(KD):
                if d % 2 == 0:
                    for n in (2 * KF + d, 2 * KF + d + 1):
                        chunk(0, n, n % 4, 16 * (n // 4) + 16)
                pool_square(pool, 1, d)
            nc.gpsimd.iota(dist[:, :], pattern=[[1, SEQ]], base=P - SEQ, channel_multiplier=-1,
                           allow_small_or_imprecise_dtypes=True).then_inc(dist_done, 1)
            pool.wait_ge(dist_done, 1)
            nc.gpsimd.affine_select(out=dist[:, :], in_=dist[:, :], compare_op=ALU.is_ge, fill=MASKED, base=SEQ - P,
                                    pattern=[[-1, SEQ]], channel_multiplier=1).then_inc(dist_done, 1)
            for r, src in enumerate((cq[:, 0, :], cq[:, 1, :], ckv[:, :])):
                pool.wait_ge(evac, r + 1)
                nc.gpsimd.tensor_tensor(lat_sq[:, r, :], src, src, ALU.mult).then_inc(lsq_done, 1)
            pool.wait_ge(is_acc, 3 * IDX_HEADS)
            for c in range(1, QT):
                d = score[:, c - 1, c * P:(c + 1) * P]
                nc.gpsimd.affine_select(out=d, in_=d, compare_op=ALU.is_ge, fill=FUTURE, base=0, pattern=[[-1, P]],
                                        channel_multiplier=1).then_inc(causal_done, 1)
            for n in (2, 3):
                for k in range(KD):
                    pool_square(pool, n, k)


_INS = ["x", "c", "w_ada", "b_ada", "g_ffn1", "w1_ffn1", "w3_ffn1", "w2_ffn1", "g_mix", "w_in", "g_cq", "g_ckv",
        "g_kidx", "b_kidx", "w_uq", "w_qidx", "w_uk", "w_uv", "w_proj_dsa", "w_proj_moba", "w_out", "g_ffn2",
        "w1_ffn2", "w3_ffn2", "w2_ffn2", "g_final"]


def kernel(**inputs):
    import numpy as _np
    import concourse.bacc as _bacc
    from concourse import mybir as _mybir
    from concourse.bass_utils import run_bass_kernel_spmd as _run

    nc = _bacc.Bacc("TRN2", target_bir_lowering=False, num_devices=1)
    arrays, args = {}, []
    for name in _INS:
        a = _np.ascontiguousarray(inputs[name])
        arrays[f"in_{name}"] = a
        args.append(nc.dram_tensor(f"in_{name}", a.shape, _mybir.dt.from_np(a.dtype), kind="ExternalInput").ap())
    args.append(nc.dram_tensor("out_x", inputs["x"].shape, _mybir.dt.float32, kind="ExternalOutput").ap())
    build_layer(nc, *args)
    r = _run(nc, [arrays], core_ids=[0])
    return r.results[0]["out_x"]
```

```python
from contextlib import ExitStack

import concourse.bass as bass
from concourse import mybir

F32 = mybir.dt.float32
F32R = mybir.dt.float32r
ALU = mybir.AluOpType
ACT = mybir.ActivationFunctionType
AX = mybir.AxisListType

P = 128
SEQ = 512
D_MODEL = 1024
D_FF = 2816
HEADS = 8
HEAD_DIM = 64
IDX_HEADS = 4
TOPK = 128
EPS = 1e-6
KD = D_MODEL // P
KF = D_FF // P
KH = KF // 2
QT = SEQ // P
HP = HEADS // 2
N_MOD = 9

RAW = 4
SPL = 2

U_UP = [0, 108]
U_DOWN = [44, 152]
U_LAT = 60
U_QKV = 64
U_GATE = 76
U_MERGE = 92
U_OUT = 100
QKV_COL = 452

R_BADA, R_G1, R_GM, R_G2, R_GF, R_CQ, R_CKV, R_C, R_GK, R_BK = 0, 72, 80, 88, 96, 104, 106, 107, 115, 116
N_ROWS = 117

ADA_FIRST = 2 * KD
ADA_GROUPS = 4
N_ADA = N_MOD * KD - ADA_FIRST
MASKED = -1.0e30
FUTURE = -3.0e38
TAKEN = -3.3e38


def build_layer(nc, x_in, c_in, w_ada, b_ada, g_ffn1, w1_ffn1, w3_ffn1, w2_ffn1, g_mix, w_in, g_cq, g_ckv,
                g_kidx, b_kidx, w_uq, w_qidx, w_uk, w_uv, w_proj_dsa, w_proj_moba, w_out, g_ffn2, w1_ffn2,
                w3_ffn2, w2_ffn2, g_final, out):
    ctx = ExitStack()
    with ctx:
        base = -(-nc.sbuf_base // 64) * 64

        def at(name, shape, offset, dt=F32):
            return nc.alloc_sbuf_tensor_at(name, [P] + shape, dt, offset=base + offset)

        raw = [at(f"raw{r}", [KH * P], r * 5632) for r in range(RAW)]
        w_hi = [at(f"w_hi{r}", [KH * P], 22528 + r * 5632, F32R) for r in range(SPL)]
        w_lo = [at(f"w_lo{r}", [KH * P], 33792 + r * 5632, F32R) for r in range(SPL)]
        xT = at("xT", [KD, SEQ], 45056)
        h_hi = at("h_hi", [KD, SEQ], 61440, F32R)
        h_lo = at("h_lo", [KD, SEQ], 77824, F32R)
        big = 94208
        g_hi = at("g_hi", [KF, SEQ], big, F32R)
        g_lo = at("g_lo", [KF, SEQ], big + 45056, F32R)
        tmp = at("tmp", [4, SEQ], big + 90112)
        nrm = at("nrm", [4, SEQ], big + 81920)
        ada = at("ada", [4, KD, P], big + 98304)
        ada0 = at("ada0", [ADA_GROUPS, KD, 4 * P], big)
        x_tok = at("x_tok", [QT, D_MODEL], big + 98304)
        dq = at("dq", [HP, SEQ], big)
        dk = at("dk", [HP, SEQ], big + 8192)
        dv = at("dv", [QT, SEQ], big + 16384)
        qi = at("qi", [2, SEQ], big + 24576)
        ki = at("ki", [SEQ], big + 28672)
        score = at("score", [3, SEQ], big + 30720)
        dist = at("dist", [SEQ], big + 36864)
        mq = at("mq", [HP, SEQ], big + 38912)
        mk = at("mk", [HP, SEQ], big + 47104)
        mv = at("mv", [QT, SEQ], big + 55296)
        mvT = at("mvT", [HP, SEQ], big + 63488)
        lat_sq = at("lat_sq", [3, SEQ], big + 63488)
        relu = at("relu", [3, SEQ], big + 63488)
        prob = at("prob", [3, SEQ], big + 63488)
        probT = at("probT", [2, SEQ], big + 69632)
        kw = at("kw", [QT, 68], big + 71680)
        max8 = at("max8", [3, 8], big + 73728)
        gate = at("gate", [2 * KD, SEQ], big + 75776)
        cq = at("cq", [2, SEQ], big + 75776)
        ckv = at("ckv", [SEQ], big + 79872)
        kiw = at("kiw", [SEQ], big + 81920)
        s_uq = at("s_uq", [2, SEQ], big + 83968)
        s_qidx = at("s_qidx", [2, 256], big + 88064)
        s_uk = at("s_uk", [SEQ], big + 90112)
        s_uv = at("s_uv", [SEQ], big + 92160)
        lat_r = at("lat_r", [2, SEQ], big + 108544)
        kn = at("kn", [QT, P], big + 112640)
        y_hi = at("y_hi", [KD, SEQ], big + 38912, F32R)
        y_lo = at("y_lo", [KD, SEQ], big + 55296, F32R)
        mrg = at("mrg", [2, 3, SEQ], big)
        out_tok = at("out_tok", [QT, D_MODEL], big + 98304)
        fin = at("fin", [2, SEQ], 61440)
        msc = big + 114688
        ident = at("ident", [P], msc)
        ones = at("ones", [P], msc + 512)
        cols = at("cols", [P], msc + 1024)
        rows = at("rows", [P], big + 81920)
        ada_acc = at("ada_acc", [2, P], msc + 1536)
        mods = at("mods", [N_MOD * KD], msc + 2560)
        c_act = at("c_act", [KD], msc + 2880)
        a_mul = at("a_mul", [3, KD], msc + 2944)
        o_mul = at("o_mul", [3, KD], msc + 3072)
        stats = at("stats", [QT, 6], msc + 3200)
        mean = at("mean", [QT, 2], msc + 3328)
        k_rstd = at("k_rstd", [QT, 2], msc + 3392)
        widx = at("widx", [QT, IDX_HEADS], msc + 3456)
        nmax = at("nmax", [4, 1], msc + 3520)
        psumq = at("psumq", [4, 1], msc + 3552)
        rsum = at("rsum", [4, 1], msc + 3584)
        eps = at("eps", [1], msc + 3616)
        warm = at("warm", [1], msc + 3648)
        rtok = at("rtok", [QT], msc + 3680)

        ps = ctx.enter_context(nc.psum_tensor("ps", [P, 8, SEQ], F32))
        B_SUM, B_MOD = 4, 5

        def sem(name):
            return ctx.enter_context(nc.semaphore(name))

        s_in = sem("s_in")
        s_rows = sem("s_rows")
        raw_in = [sem(f"raw_in{r}") for r in range(RAW)]
        hi_done = sem("hi_done")
        lo_done = sem("lo_done")
        unit_done = sem("unit_done")
        silu_done = sem("silu_done")
        g_done = sem("g_done")
        ghi_done = sem("ghi_done")
        glo_done = sem("glo_done")
        x_done = sem("x_done")
        sq_done = sem("sq_done")
        acc_done = sem("acc_done")
        sum_done = sem("sum_done")
        sqrt_done = sem("sqrt_done")
        rstd_done = sem("rstd_done")
        u_done = sem("u_done")
        hhi_done = sem("hhi_done")
        hlo_done = sem("hlo_done")
        ada0_in = [sem(f"ada0_in{r}") for r in range(ADA_GROUPS)]
        ada_in = [sem(f"ada_in{r}") for r in range(4)]
        ada_step = sem("ada_step")
        ada_sum = sem("ada_sum")
        ada_used = sem("ada_used")
        ada0_sum = sem("ada0_sum")
        dve_ada = sem("dve_ada")
        const_done = sem("const_done")
        const_step = sem("const_step")
        mod0_done = sem("mod0_done")
        cols_psum = sem("cols_psum")
        cols_done = sem("cols_done")
        cact_done = sem("cact_done")
        xt_psum = sem("xt_psum")
        mod_done = sem("mod_done")
        mods_all = sem("mods_all")
        evac = sem("evac")
        small_in = sem("small_in")
        lsq_done = sem("lsq_done")
        lat_psum = sem("lat_psum")
        lat_dve = sem("lat_dve")
        lat_act = sem("lat_act")
        kn_psum = sem("kn_psum")
        prj_psum = sem("prj_psum")
        prj_free = sem("prj_free")
        is_psum = sem("is_psum")
        is_relu = sem("is_relu")
        is_acc = sem("is_acc")
        vt_psum = sem("vt_psum")
        vt_done = sem("vt_done")
        causal_done = sem("causal_done")
        dist_done = sem("dist_done")
        tk_step = sem("tk_step")
        s_psum = sem("s_psum")
        s_used = sem("s_used")
        m_done = sem("m_done")
        e_done = sem("e_done")
        r_done = sem("r_done")
        p_done = sem("p_done")
        pt_psum = sem("pt_psum")
        pt_done = sem("pt_done")
        pv_done = sem("pv_done")
        ohi_done = sem("ohi_done")
        olo_done = sem("olo_done")
        mg_step = sem("mg_step")
        mg_free = sem("mg_free")
        mg_y = sem("mg_y")
        yhi_done = sem("yhi_done")
        ylo_done = sem("ylo_done")
        fin_done = sem("fin_done")
        fin_psum = sem("fin_psum")
        fin_tok = sem("fin_tok")
        fin_act = sem("fin_act")
        fin_dve = sem("fin_dve")
        s_out = sem("s_out")

        def ktiles(w):
            return w.rearrange("(k p) n -> p k n", p=P)

        w_up = [[ktiles(w1_ffn1[0]), ktiles(w3_ffn1[0])], [ktiles(w1_ffn2[0]), ktiles(w3_ffn2[0])]]
        w_dn = [ktiles(w2_ffn1[0]), ktiles(w2_ffn2[0])]
        w_in_v, w_out_v = ktiles(w_in[0]), ktiles(w_out[0])
        w_pd_v, w_pm_v = ktiles(w_proj_dsa[0]), ktiles(w_proj_moba[0])
        w_ada_v = ktiles(w_ada[0])

        def nk_of(u):
            return KH if U_DOWN[0] <= u < U_LAT or u >= U_DOWN[1] else KD

        N_UNITS = U_DOWN[1] + 2 * KD

        def done(u):
            return u + 1 + SPL

        def split(u):
            return u + 1 + RAW

        def load_unit(sp, u, j, first, second, nk):
            sp.wait_ge(lo_done, u + 1)
            dst = raw[j][:, 0:nk * P].rearrange("p (k n) -> p k n", k=nk)
            m = first.shape[1]
            sp.dma_start(dst[:, 0:m], first).then_inc(raw_in[j], 16)
            sp.dma_start(dst[:, m:nk], second).then_inc(raw_in[j], 16)

        def load_cols(sp, u, j, w, col, k0, nk):
            m = nk // 2
            load_unit(sp, u, j, w[:, k0:k0 + m, bass.ds(col, P)], w[:, k0 + m:k0 + nk, bass.ds(col, P)], nk)

        def arrivals(u4):
            return 32 * (u4 + 1)

        def split_hi(act, u4, j, nk):
            act.wait_ge(raw_in[j], arrivals(u4))
            act.wait_ge(unit_done, 4 * u4 + j + 1)
            nc.scalar.activation(w_hi[j % SPL][:, 0:nk * P], raw[j][:, 0:nk * P], ACT.Copy).then_inc(hi_done, 1)

        def split_lo(dve, u4, j, nk):
            dve.wait_ge(hi_done, 4 * u4 + j + 1)
            nc.vector.tensor_tensor(w_lo[j % SPL][:, 0:nk * P], raw[j][:, 0:nk * P],
                                    w_hi[j % SPL][:, 0:nk * P].bitcast(F32), ALU.subtract).then_inc(lo_done, 1)

        def hi_u(act, u):
            if u < N_UNITS:
                split_hi(act, u // 4, u % 4, nk_of(u))

        def lo_u(dve, u):
            if u < N_UNITS:
                split_lo(dve, u // 4, u % 4, nk_of(u))

        def mm3(bank, j, kk, rhs_hi, rhs_lo, start, stop):
            hi = w_hi[j % SPL][:, kk * P:(kk + 1) * P]
            lo = w_lo[j % SPL][:, kk * P:(kk + 1) * P]
            nc.tensor.matmul(ps[:, bank, :], hi, rhs_hi, start=start, stop=False)
            nc.tensor.matmul(ps[:, bank, :], hi, rhs_lo, start=False, stop=False)
            return nc.tensor.matmul(ps[:, bank, :], lo, rhs_hi, start=False, stop=stop)

        def unit(bank, j, rhs_hi, rhs_lo, nk=KD, k0=0, start=True, stop=True):
            for kk in range(nk):
                last = mm3(bank, j, kk, rhs_hi[:, k0 + kk, :], rhs_lo[:, k0 + kk, :],
                           start and kk == 0, stop and kk == nk - 1)
            return last

        def act_square(act, n, k):
            act.wait_ge(x_done, KD * n + k + 1)
            if k >= 2:
                act.wait_ge(acc_done, 6 * n + k - 1)
            nc.scalar.activation(tmp[:, k % 2, :], xT[:, k, :], ACT.Square).then_inc(sq_done, 1)

        def dve_square_sum(dve, n, k):
            if not 1 <= k < KD - 1:
                return
            dve.wait_ge(sq_done, KD * n + k + 1)
            if k > 1:
                dve.wait_ge(acc_done, 6 * n + k - 1)
            nc.vector.tensor_tensor(tmp[:, 2, :], tmp[:, 2 if k > 1 else 0, :], tmp[:, k % 2, :], ALU.add)\
                .then_inc(acc_done, 1)

        def pe_sum(pe, n):
            pe.wait_ge(acc_done, 6 * (n + 1))
            nc.tensor.matmul(ps[:, B_SUM, :], ones[:, :], tmp[:, 2, :], start=True, stop=False)
            pe.wait_ge(sq_done, KD * (n + 1))
            nc.tensor.matmul(ps[:, B_SUM, :], ones[:, :], tmp[:, (KD - 1) % 2, :], start=False, stop=True)\
                .then_inc(sum_done, 1)

        def act_warm(act, func):
            act.wait_ge(const_done, 2)
            nc.scalar.activation(warm[:, :], eps[:, :], func)

        def act_sqrt(act, n):
            act.wait_ge(sum_done, n + 1)
            nc.scalar.activation(tmp[:, 3, :], ps[:, B_SUM, :], ACT.Sqrt, bias=eps[:, :], scale=1.0 / D_MODEL)\
                .then_inc(sqrt_done, 1)

        def dve_rstd(dve, n):
            dve.wait_ge(sqrt_done, n + 1)
            nc.vector.reciprocal(tmp[:, 3, :], tmp[:, 3, :]).then_inc(rstd_done, 1)
            dve.wait_ge(rstd_done, n + 1)

        def dve_scaled(n, k):
            nc.vector.scalar_tensor_tensor(nrm[:, k % 4, :], tmp[:, 3, :], a_mul[:, n, k:k + 1], xT[:, k, :],
                                           ALU.mult, ALU.mult).then_inc(u_done, 1)

        def dve_low(dve, n, k):
            dve.wait_ge(hhi_done, KD * n + k + 1)
            nc.vector.scalar_tensor_tensor(h_lo[:, k, :], nrm[:, k % 4, :], mods[:, 24 * n + k:24 * n + k + 1],
                                           h_hi[:, k, :].bitcast(F32), ALU.add, ALU.subtract).then_inc(hlo_done, 1)

        def dve_h(dve, n):
            dve_rstd(dve, n)
            dve_scaled(n, 0)
            for k in range(1, KD):
                dve_scaled(n, k)
                dve_low(dve, n, k - 1)
            dve_low(dve, n, KD - 1)

        def act_h(act, n):
            act_sqrt(act, n)
            for k in range(KD):
                act.wait_ge(u_done, KD * n + k + 1)
                nc.scalar.activation(h_hi[:, k, :], nrm[:, k % 4, :], ACT.Identity,
                                     bias=mods[:, 24 * n + k:24 * n + k + 1]).then_inc(hhi_done, 1)

        def sp_ffn(sp, f):
            with sp.Fori(0, KF // 2) as i:
                for j in range(4):
                    load_cols(sp, U_UP[f] + 4 * i + j, j, w_up[f][j % 2], i * (2 * P) + (j // 2) * P, 0, KD)
            with sp.Fori(0, KD // 2) as i:
                for j in range(4):
                    load_cols(sp, U_DOWN[f] + 4 * i + j, j, w_dn[f], i * (2 * P) + (j // 2) * P, (j % 2) * KH, KH)

        def pe_ada(pe, n, slot):
            pe.wait_ge(ada_sum, n + 1)
            nc.tensor.matmul(ps[:, B_MOD, bass.ds(n + ADA_FIRST, 1)], ada_acc[:, slot, :], ones[:, 0:1],
                             start=True, stop=True).then_inc(ada_used, 1)

        def pe_first_pair(pe, u, n, banks):
            pe.wait_ge(lo_done, split(u + 1))
            for kk in range(KD):
                pe.wait_ge(hlo_done, KD * n + kk + 1)
                for q in range(2):
                    last = mm3(banks[q], u + q, kk, h_hi[:, kk, :], h_lo[:, kk, :], kk == 0, kk == KD - 1)
                    if kk == KD - 1:
                        last.then_inc(unit_done, 1)

        def pe_ffn(pe, f):
            def up(i, j):
                pe.wait_ge(lo_done, U_UP[f] + 4 * i + j + 1 + RAW)
                if j % 2 == 0:
                    pe.wait_ge(g_done, KF * f + 2 * i + j // 2 + 1)
                unit(j, j, h_hi, h_lo).then_inc(unit_done, 1)

            pe_first_pair(pe, U_UP[f], 2 * f, (0, 1))
            for j in range(4):
                if j >= 2:
                    up(0, j)
                if f == 0 and j:
                    pe_ada(pe, j - 1, (j - 1) % 2)
            with pe.Fori(1, KF // 2) as i:
                for j in range(4):
                    up(i, j)
                    if f == 0:
                        pe_ada(pe, 4 * i + j - 1, (j - 1) % 2)
            if f == 0:
                pe_ada(pe, 2 * KF - 1, 1)

            def down(i, with_ada, tiles):
                for j in range(4):
                    pe.wait_ge(lo_done, U_DOWN[f] + 4 * i + j + 1 + RAW)
                    if j % 2 == 0:
                        pe.wait_ge(g_done, KF * (f + 1) + 1)
                        pe.wait_ge(x_done, KD * (1 + 2 * f) + 2 * i + j // 2 - 1)
                    pe.wait_ge(glo_done, KF * f + KH * (j % 2 + 1))
                    unit(j // 2, j, g_hi, g_lo, nk=KH, k0=KH * (j % 2), start=j % 2 == 0, stop=j % 2 == 1)\
                        .then_inc(unit_done, 1)
                    if with_ada:
                        pe.wait_ge(mod_done, 1)
                        pe_ada(pe, 2 * KF + 4 * i + j, j % 2)
                    if j in tiles:
                        pe_token_major(pe, 2 * i + j // 2 - 1, (j // 2 + 1) % 2)

            if f == 0:
                with pe.Fori(0, KD // 2 - 1) as i:
                    down(i, True, ())
                down(KD // 2 - 1, False, ())
            else:
                down(0, False, (2,))
                with pe.Fori(1, KD // 2) as i:
                    down(i, False, (0, 2))
                pe_token_major(pe, KD - 1, (KD - 1) % 2)

        def pe_token_major(pe, d, slot):
            pe.wait_ge(fin_done, d + 1)
            pe.wait_ge(g_done, 2 * KF + 2)
            for t in range(QT):
                last = nc.tensor.transpose(ps[:, 2 + slot, t * P:(t + 1) * P], fin[:, slot, t * P:(t + 1) * P], ident[:, :])
            last.then_inc(fin_psum, 1)

        def act_pair(act, f, i, jp, nk):
            u = U_UP[f] + 4 * i + 2 * jp
            pair = KF * f + 2 * i + jp
            split_hi(act, U_UP[f] // 4 + i + (jp == 1), (2 * jp + 2) % 4, nk)
            act.wait_ge(unit_done, u + 1 + SPL)
            act.wait_ge(g_done, pair + 1)
            nc.scalar.activation(tmp[:, jp, :], ps[:, 2 * jp, :], ACT.Silu).then_inc(silu_done, 1)
            split_hi(act, U_UP[f] // 4 + i + (jp == 1), (2 * jp + 3) % 4, nk)
            act.wait_ge(g_done, pair + 1 + 2)
            nc.scalar.activation(g_hi[:, bass.ds(2 * i + jp, 1), :], tmp[:, 2 + jp:3 + jp, :],
                                 ACT.Copy).then_inc(ghi_done, 1)
            if f == 0:
                for j in (2 * jp, 2 * jp + 1):
                    act_ada(act, 4 * i + j + 4, j)

        def act_ada(act, n, slot):
            if not isinstance(n, int) or n >= 4:
                act.wait_ge(ada_sum, n - 3)
            act.dma_start(ada[:, slot], w_ada_v[:, :, bass.ds(n * P + ADA_FIRST * P, P)]).then_inc(ada_in[slot], 16)

        def dve_pair(dve, f, i, jp, nk):
            pair = KF * f + 2 * i + jp
            for q in (2, 3):
                split_lo(dve, U_UP[f] // 4 + i + (jp == 1), (2 * jp + q) % 4, nk)
            dve.wait_ge(silu_done, pair + 1)
            dve.wait_ge(unit_done, U_UP[f] + 4 * i + 2 * jp + 2 + SPL)
            nc.vector.tensor_tensor(tmp[:, 2 + jp, :], tmp[:, jp, :], ps[:, 2 * jp + 1, :],
                                    ALU.mult).then_inc(g_done, 1)
            dve.wait_ge(ghi_done, pair + 1)
            nc.vector.tensor_tensor(g_lo[:, bass.ds(2 * i + jp, 1), :], tmp[:, 2 + jp:3 + jp, :],
                                    g_hi[:, bass.ds(2 * i + jp, 1), :].bitcast(F32), ALU.subtract).then_inc(glo_done, 1)

        def pairs(eng, f, step):
            with eng.Fori(0, KF // 2 - 1) as i:
                step(eng, f, i, 0, KD)
                step(eng, f, i, 1, KD)
            step(eng, f, KF // 2 - 1, 0, KD)
            step(eng, f, KF // 2 - 1, 1, KH)

        def act_down(act, f):
            for d in range(KD):
                hi_u(act, U_DOWN[f] + 2 * d + 2)
                if f == 0 and d < 4:
                    act_ada(act, 2 * KF + 4 + 2 * d, (2 * d) % 4)
                    act_ada(act, 2 * KF + 5 + 2 * d, (2 * d + 1) % 4)
                if d == KD - 1:
                    act_warm(act, ACT.Sqrt)
                act_square(act, 1 + 2 * f, d)
                if f:
                    act_final(act, d)
                hi_u(act, U_DOWN[f] + 2 * d + 3)

        def act_final(act, d):
            if d >= 2:
                act.wait_ge(fin_psum, d - 1)
            nc.scalar.activation(fin[:, d % 2, :], xT[:, d, :], ACT.Copy, scale=cols[:, R_GF + d:R_GF + d + 1])\
                .then_inc(fin_done, 1)
            if d:
                act_token_major(act, d - 1)

        def act_token_major(act, d):
            act.wait_ge(fin_psum, d + 1)
            nc.scalar.activation(out_tok[:, :, d * P:(d + 1) * P], ps[:, 2 + d % 2, :].rearrange("p (t n) -> p t n", t=QT),
                                 ACT.Copy).then_inc(fin_tok, 1)

        def residual(dve, n, d, bank):
            nc.vector.scalar_tensor_tensor(xT[:, d, :], ps[:, bank, :], o_mul[:, n, d:d + 1], xT[:, d, :],
                                           ALU.mult, ALU.add).then_inc(x_done, 1)

        def dve_down(dve, f):
            if f == 0:
                dve_gate(dve)
            for d in range(KD):
                lo_u(dve, U_DOWN[f] + 2 * d + 2)
                dve.wait_ge(unit_done, done(U_DOWN[f] + 2 * d + 1))
                residual(dve, 2 * f, d, d % 2)
                dve_square_sum(dve, 1 + 2 * f, d - 1)
                lo_u(dve, U_DOWN[f] + 2 * d + 3)

        def dve_gate(dve):
            dve.wait_ge(ada_used, 2 + 2 * KF)
            nc.vector.tensor_tensor(mods[:, 16:24], ps[:, B_MOD, 16:24], cols[:, 16:24], ALU.add).then_inc(mod_done, 1)
            dve.wait_ge(mod_done, 1)
            nc.vector.tensor_scalar(o_mul[:, 0, :], mods[:, 16:24], 0.5, 0.5, ALU.mult, ALU.add).then_inc(mod_done, 1)
            dve.wait_ge(mod_done, 2)

        def dve_mods(dve):
            dve.wait_ge(ada_used, 2 + N_MOD * KD - ADA_FIRST)
            nc.vector.tensor_tensor(mods[:, 24:72], ps[:, B_MOD, 24:72], cols[:, 24:72], ALU.add).then_inc(mod_done, 1)
            dve.wait_ge(mod_done, 3)
            nc.vector.tensor_scalar(o_mul[:, 1, :], mods[:, 40:48], 1.0, None, ALU.add).then_inc(mod_done, 1)
            nc.vector.tensor_scalar(o_mul[:, 2, :], mods[:, 64:72], 0.5, 0.5, ALU.mult, ALU.add).then_inc(mod_done, 1)
            for n, r in ((1, R_GM), (2, R_G2)):
                nc.vector.scalar_tensor_tensor(a_mul[:, n, :], mods[:, 24 * n + 8:24 * n + 16], 1.0, cols[:, r:r + KD],
                                               ALU.add, ALU.mult).then_inc(mod_done, 1)
            dve.wait_ge(mod_done, 7)

        steps = [(b, hp, e, c) for b in range(2) for hp in range(HP) for e in range(2) for c in range(QT)]
        NST = len(steps)
        B_S, B_T, B_O = (0, 1), (2, 3), (6, 7)

        block = ctx.enter_context(nc.Block())

        @block.sync
        def _(sp):
            for r, src in ((R_BADA, b_ada), (R_G1, g_ffn1), (R_GM, g_mix), (R_G2, g_ffn2), (R_CQ, g_cq), (R_CKV, g_ckv),
                           (R_C, c_in)):
                v = src[0].rearrange("(r n) -> r n", n=P)
                sp.dma_start(rows[r:r + v.shape[0], :], v).then_inc(s_rows, 16)
            sp.dma_start(rows[R_GF:R_GF + KD, :], g_final.rearrange("(r n) -> r n", n=P)).then_inc(s_rows, 16)
            for r, src in ((R_GK, g_kidx), (R_BK, b_kidx)):
                for half in range(2):
                    sp.dma_start(rows[r:r + 1, 64 * half:64 * half + 64], src).then_inc(s_rows, 16)
            for t in range(QT):
                sp.dma_start(x_tok[:, t, :], x_in[0, t * P:(t + 1) * P, :]).then_inc(s_in, 16)
            for r in range(ADA_GROUPS):
                for half in range(2):
                    c = half * D_MODEL + r * 2 * P
                    sp.dma_start(ada0[:, r, :, half * 2 * P:(half + 1) * 2 * P], w_ada_v[:, :, c:c + 2 * P])\
                        .then_inc(ada0_in[r], 16)
            sp_ffn(sp, 0)
            for q in range(4):
                load_cols(sp, U_LAT + q, q, w_in_v, q * P, 0, KD)
            for q in range(4):
                load_cols(sp, U_QKV + q, q, w_in_v, QKV_COL + q * P, 0, KD)
            sp.wait_ge(unit_done, done(U_LAT - 1))
            sp.dma_start(s_uq[:], w_uq[0].rearrange("(k p) h d -> p k (h d)", p=P)).then_inc(small_in, 16)
            sp.dma_start(s_qidx[:], w_qidx[0].rearrange("(k p) h d -> p k (h d)", p=P)).then_inc(small_in, 16)
            sp.dma_start(s_uk[:], w_uk[0].rearrange("p h d -> p (h d)")).then_inc(small_in, 16)
            sp.dma_start(s_uv[:], w_uv[0].rearrange("p h d -> p (h d)")).then_inc(small_in, 16)
            with sp.Fori(0, 6) as i:
                for j in range(4):
                    load_cols(sp, U_QKV + 4 + 4 * i + j, j, w_in_v, i * (4 * P) + (QKV_COL + (4 + j) * P), 0, KD)
            for q in range(KD):
                load_unit(sp, U_MERGE + q, q % 4, w_pd_v[:, :, q * P:(q + 1) * P], w_pm_v[:, :, q * P:(q + 1) * P], KD)
            for q in range(KD):
                load_cols(sp, U_OUT + q, q % 4, w_out_v, q * P, 0, KD)
            sp_ffn(sp, 1)
            for t in range(QT):
                sp.wait_ge(fin_act if t % 2 == 0 else fin_dve, t // 2 + 1)
                sp.dma_start(out[0, t * P:(t + 1) * P, :], out_tok[:, t, :]).then_inc(s_out, 16)
            sp.wait_ge(s_out, 16 * QT)

        @block.tensor
        def _(pe):
            pe.sem_inc(unit_done, SPL)
            pe.sem_inc(ada_used, 2)
            pe.wait_ge(s_rows, 16 * 12)
            pe.wait_ge(const_done, 2)
            nc.tensor.transpose(ps[:, B_MOD, 0:N_ROWS], rows[0:N_ROWS, :], ident[0:N_ROWS, 0:N_ROWS]).then_inc(cols_psum, 1)
            pe.wait_ge(s_in, 16 * QT)
            for k in range(KD):
                bank = (0, 1, 2, 3)[k % 4]
                if k >= 4:
                    pe.wait_ge(x_done, k - 3)
                for t in range(QT):
                    last = nc.tensor.transpose(ps[:, bank, t * P:(t + 1) * P], x_tok[:, t, k * P:(k + 1) * P], ident[:, :])
                last.then_inc(xt_psum, 1)
            pe_sum(pe, 0)
            for r in range(ADA_GROUPS):
                pe.wait_ge(dve_ada, KD * (r + 1))
                if r:
                    pe.wait_ge(mod0_done, 3 * r)
                for q in range(4):
                    n = (q // 2) * KD + 2 * r + q % 2
                    last = nc.tensor.matmul(ps[:, B_MOD, n:n + 1], ada0[:, r, KD - 1, q * P:(q + 1) * P], ones[:, 0:1],
                                            start=True, stop=True)
                last.then_inc(ada0_sum, 1)
            pe.wait_ge(mod0_done, 3 * ADA_GROUPS)
            pe_ffn(pe, 0)
            pe_sum(pe, 1)

            def single(u):
                pe.wait_ge(lo_done, split(u))
                if u >= U_LAT + 4:
                    pe.wait_ge(evac, u - U_LAT - 3)
                for kk in range(KD):
                    last = mm3(u % 4, u, kk, h_hi[:, kk, :], h_lo[:, kk, :], kk == 0, kk == KD - 1)
                last.then_inc(unit_done, 1)

            pe_first_pair(pe, U_LAT, 1, (0, 1))
            single(U_LAT + 2)
            single(U_LAT + 3)
            single(U_QKV)
            single(U_QKV + 1)
            pe.wait_ge(lsq_done, 3)
            nc.tensor.matmul(ps[:, 4, :], ones[:, :], lat_sq[:, 0, :], start=True, stop=False)
            nc.tensor.matmul(ps[:, 4, :], ones[:, :], lat_sq[:, 1, :], start=False, stop=True).then_inc(lat_psum, 1)
            nc.tensor.matmul(ps[:, 6, :], ones[:, :], lat_sq[:, 2, :], start=True, stop=True).then_inc(lat_psum, 1)
            pe.wait_ge(evac, 4)
            for t in range(QT):
                last = nc.tensor.transpose(ps[:, 7, t * 68:(t + 1) * 68], kiw[0:68, t * P:(t + 1) * P], ident[0:68, 0:68])
            last.then_inc(lat_psum, 1)
            for q in range(2, 6):
                single(U_QKV + q)
            pe.wait_ge(lat_dve, 17)
            for t in range(QT):
                last = nc.tensor.transpose(ps[:, 7, t * P:(t + 1) * P], kn[:, t, :], ident[:, :])
            last.then_inc(kn_psum, 1)
            pe.wait_ge(small_in, 64)
            for n in range(14):
                bank = 4 + n % 3
                if n >= 3:
                    pe.wait_ge(prj_free, n - 2)
                if n < 6:
                    for r in range(2):
                        w = s_qidx[:, r, n * P:(n + 1) * P] if n < 2 else s_uq[:, r, (n - 2) * P:(n - 1) * P]
                        last = nc.tensor.matmul(ps[:, bank, :], w, cq[:, r, :], start=r == 0, stop=r == 1)
                elif n < 10:
                    last = nc.tensor.matmul(ps[:, bank, :], s_uk[:, (n - 6) * P:(n - 5) * P], ckv[:, :], start=True, stop=True)
                else:
                    last = nc.tensor.matmul(ps[:, bank, :], ckv[:, (n - 10) * P:(n - 9) * P], s_uv[:, :], start=True, stop=True)
                last.then_inc(prj_psum, 1)
            for q in range(6, 12):
                single(U_QKV + q)
            pe.wait_ge(evac, 16)
            for t in range(QT):
                bank = (7, 4, 5, 6)[t]
                if t == 0:
                    pe.wait_ge(lat_dve, 18)
                if t == 1:
                    pe.wait_ge(prj_free, 14)
                for hp in range(HP):
                    last = nc.tensor.transpose(ps[:, bank, hp * P:(hp + 1) * P], mvT[:, hp, t * P:(t + 1) * P], ident[:, :])
                last.then_inc(vt_psum, 1)
            pe.wait_ge(vt_done, 4)
            n = 0
            for c in range(1, QT):
                for h in range(IDX_HEADS):
                    if n >= 3:
                        pe.wait_ge(is_relu, n - 2)
                    o = 64 * (h % 2)
                    nc.tensor.matmul(ps[:, 4 + n % 3, 0:(c + 1) * P], qi[o:o + 64, h // 2, c * P:(c + 1) * P],
                                     ki[o:o + 64, 0:(c + 1) * P], start=True, stop=True).then_inc(is_psum, 1)
                    n += 1
            with pe.Fori(0, 4) as i:
                for j in range(4):
                    pe.wait_ge(lo_done, U_GATE + 4 * i + j + 1 + RAW)
                    pe.wait_ge(evac, U_GATE - U_LAT - 3 + 4 * i + j)
                    unit(j, j, h_hi, h_lo).then_inc(unit_done, 1)
            pe.wait_ge(evac, 32)

            def scores(n):
                b, hp, e, c = steps[n]
                q, k = ((mq, mk), (dq, dk))[b]
                if n >= 2:
                    pe.wait_ge(s_used, n - 1)
                o = 64 * e
                nc.tensor.matmul(ps[:, B_S[n % 2], 0:(c + 1) * P], q[o:o + 64, hp, c * P:(c + 1) * P],
                                 k[o:o + 64, hp, 0:(c + 1) * P], start=True, stop=True).then_inc(s_psum, 1)

            def transposes(n):
                c = steps[n][3]
                pe.wait_ge(p_done, n + 1)
                if n >= 2:
                    pe.wait_ge(pt_done, n - 1)
                for s in range(c + 1):
                    last = nc.tensor.transpose(ps[:, B_T[n % 2], s * P:(s + 1) * P], prob[:, n % 3, s * P:(s + 1) * P], ident[:, :])
                last.then_inc(pt_psum, 1)

            def values(n):
                b, hp, e, c = steps[n]
                v = (mv, dv)[b]
                pair = HP * b + hp
                pe.wait_ge(pt_done, n + 1)
                if pair >= 2 and e == 0 and c == 0:
                    pe.wait_ge(olo_done, pair - 1)
                for s in range(c + 1):
                    last = nc.tensor.matmul(ps[64 * e:64 * e + 64, B_O[pair % 2], c * P:(c + 1) * P],
                                            v[:, s, hp * P + 64 * e:hp * P + 64 * e + 64], probT[:, n % 2, s * P:(s + 1) * P],
                                            start=s == 0, stop=s == c)
                last.then_inc(pv_done, 1)

            for n in range(NST + 3):
                if n < NST:
                    scores(n)
                if 2 <= n < NST + 2:
                    transposes(n - 2)
                if n >= 3:
                    values(n - 3)
            for q in range(KD):
                pe.wait_ge(lo_done, split(U_MERGE + q))
                if q >= 2:
                    pe.wait_ge(mg_free, 2 * (q - 1))
                for half in range(2):
                    for kk in range(HP):
                        tile = (1 - half) * HP + kk
                        pe.wait_ge(olo_done, 2 * HP if half == 0 else HP)
                        last = mm3(2 * (q % 2) + half, q, half * HP + kk, h_hi[:, tile, :], h_lo[:, tile, :], kk == 0, kk == HP - 1)
                last.then_inc(unit_done, 1)
            for q in range(KD):
                u = U_OUT + q
                pe.wait_ge(lo_done, split(u))
                if q < 4:
                    pe.wait_ge(mg_free, 2 * KD if q >= 2 else 2 * KD - 2)
                else:
                    pe.wait_ge(x_done, 2 * KD + q - 3)
                for kk in range(KD):
                    if q == 0:
                        pe.wait_ge(ylo_done, kk + 1)
                    last = mm3(q % 4, u, kk, y_hi[:, kk, :], y_lo[:, kk, :], kk == 0, kk == KD - 1)
                last.then_inc(unit_done, 1)
            pe_sum(pe, 2)
            pe_ffn(pe, 1)
            pe.wait_ge(acc_done, 6 * 4)
            pe.wait_ge(sq_done, KD * 4)
            for t in range(QT):
                nc.tensor.matmul(ps[:, B_SUM, t:t + 1], tmp[:, 2, t * P:(t + 1) * P], ones[:, 0:1], start=True, stop=False)
                last = nc.tensor.matmul(ps[:, B_SUM, t:t + 1], tmp[:, (KD - 1) % 2, t * P:(t + 1) * P], ones[:, 0:1],
                                        start=False, stop=True)
            last.then_inc(sum_done, 1)

        @block.scalar
        def _(act):
            act.wait_ge(cols_done, 1)
            nc.scalar.activation(c_act[:, :], cols[:, R_C:R_C + KD], ACT.Silu).then_inc(cact_done, 1)
            for k in range(KD):
                act.wait_ge(xt_psum, k + 1)
                nc.scalar.activation(xT[:, k, :], ps[:, k % 4, :], ACT.Copy).then_inc(x_done, 1)
                if k:
                    act_square(act, 0, k - 1)
            act_square(act, 0, KD - 1)
            act_sqrt(act, 0)
            hi_u(act, 0)
            hi_u(act, 1)
            for k in range(KD):
                act.wait_ge(u_done, k + 1)
                nc.scalar.activation(h_hi[:, k, :], nrm[:, k % 4, :], ACT.Identity, bias=mods[:, k:k + 1]).then_inc(hhi_done, 1)
                if k == 3:
                    for n in range(4):
                        act_ada(act, n, n)
            pairs(act, 0, act_pair)
            act_down(act, 0)
            act_h(act, 1)

            def copy_out(u, dst, func=ACT.Copy, scale=1.0):
                act.wait_ge(unit_done, done(u))
                nc.scalar.activation(dst, ps[:, u % 4, :], func, scale=scale).then_inc(evac, 1)

            lat = [cq[:, 0, :], cq[:, 1, :], ckv[:, :], kiw[:, :]]
            for q in range(16):
                u = U_LAT + q
                hi_u(act, u + 2)
                if q < 4:
                    copy_out(u, lat[q])
                else:
                    hp = (q - 4) % HP
                    dst = (mq, mk, mvT)[(q - 4) // HP]
                    if q == 12:
                        act.wait_ge(lat_psum, 3)
                    copy_out(u, dst[:, hp, :], scale=HEAD_DIM ** -0.5 if q < 8 else 1.0)
                if q == 6:
                    for n, (buf, cnt) in enumerate(((lat_r[:, 0, :], 1), (lat_r[:, 1, :], 2), (k_rstd[:, :, 0], 12))):
                        act.wait_ge(lat_dve, cnt)
                        nc.scalar.activation(buf, buf, ACT.Sqrt).then_inc(lat_act, 1)
            n = 0
            for c in range(1, QT):
                for h in range(IDX_HEADS):
                    act.wait_ge(is_psum, n + 1)
                    if n >= 3:
                        act.wait_ge(is_acc, n - 2)
                    else:
                        act.wait_ge(vt_psum, 4)
                    nc.scalar.activation(relu[:, n % 3, 0:(c + 1) * P], ps[:, 4 + n % 3, 0:(c + 1) * P], ACT.Relu,
                                         scale=(IDX_HEADS * 64) ** -0.5).then_inc(is_relu, 1)
                    n += 1
            with act.Fori(0, 3) as i:
                for j in range(4):
                    split_hi(act, U_GATE // 4 + i + (j >= 2), (j + 2) % 4, KD)
                    act.wait_ge(unit_done, U_GATE + 4 * i + j + 1 + SPL)
                    nc.scalar.activation(gate[:, bass.ds(4 * i + j, 1), :], ps[:, j:j + 1, :], ACT.Sigmoid).then_inc(evac, 1)
            for q in range(12, 16):
                hi_u(act, U_GATE + q + 2)
                act.wait_ge(unit_done, done(U_GATE + q))
                nc.scalar.activation(gate[:, q, :], ps[:, q % 4, :], ACT.Sigmoid).then_inc(evac, 1)

            def exps(n):
                c = steps[n][3]
                act.wait_ge(m_done, n + 1)
                nc.scalar.activation(prob[:, n % 3, 0:(c + 1) * P], prob[:, n % 3, 0:(c + 1) * P], ACT.Exp,
                                     bias=nmax[:, n % 4, :], accum_out=psumq[:, n % 4, :]).then_inc(e_done, 1)

            def copies(n):
                c = steps[n][3]
                act.wait_ge(pt_psum, n + 1)
                if n >= 2:
                    act.wait_ge(pv_done, n - 1)
                nc.scalar.activation(probT[:, n % 2, 0:(c + 1) * P], ps[:, B_T[n % 2], 0:(c + 1) * P], ACT.Copy)\
                    .then_inc(pt_done, 1)

            def o_high(pair):
                act.wait_ge(pv_done, 8 * (pair + 1))
                nc.scalar.activation(h_hi[:, pair, :], ps[:, B_O[pair % 2], :], ACT.Copy).then_inc(ohi_done, 1)

            for n in range(NST + 4):
                if n < NST:
                    exps(n)
                if 2 <= n < NST + 2:
                    copies(n - 2)
                if n >= 11 and (n - 11) % 8 == 0:
                    o_high((n - 11) // 8)
            for q in range(KD):
                hi_u(act, U_MERGE + q + 2)
                act.wait_ge(mg_y, q + 1)
                nc.scalar.activation(y_hi[:, q, :], mrg[:, q % 2, 2, :], ACT.Copy).then_inc(yhi_done, 1)
            for q in range(KD):
                if q == KD - 1:
                    act_warm(act, ACT.Sqrt)
                act_square(act, 2, q)
                hi_u(act, U_OUT + q + 2)
            act_h(act, 2)
            pairs(act, 1, act_pair)
            act_down(act, 1)
            act.wait_ge(sum_done, 4)
            nc.scalar.activation(rtok[:, :], ps[:, B_SUM, 0:QT], ACT.Sqrt, bias=eps[:, :], scale=1.0 / D_MODEL)\
                .then_inc(sqrt_done, 1)
            act_token_major(act, KD - 1)
            act.wait_ge(rstd_done, 4)
            act.wait_ge(fin_tok, KD)
            for t in (0, 2):
                nc.scalar.activation(out_tok[:, t, :], out_tok[:, t, :], ACT.Copy, scale=rtok[:, t:t + 1]).then_inc(fin_act, 1)

        @block.vector
        def _(dve):
            dve.sem_inc(lo_done, RAW)
            dve.sem_inc(g_done, 2)
            dve.sem_inc(tk_step, 3)
            nc.vector.memset(eps[:, :], EPS)
            nc.vector.memset(ones[:, :], 1.0).then_inc(const_done, 1)
            dve.wait_ge(cols_psum, 1)
            nc.vector.tensor_copy(cols[:, 0:N_ROWS], ps[:, B_MOD, 0:N_ROWS]).then_inc(cols_done, 1)
            dve.wait_ge(cact_done, 1)
            for k in range(1, KD - 1):
                dve_square_sum(dve, 0, k)
            for r in range(ADA_GROUPS):
                dve.wait_ge(ada0_in[r], 32)
                nc.vector.tensor_scalar(ada0[:, r, 0, :], ada0[:, r, 0, :], c_act[:, 0:1], None, ALU.mult).then_inc(dve_ada, 1)
                for k in range(1, KD):
                    dve.wait_ge(dve_ada, KD * r + k)
                    nc.vector.scalar_tensor_tensor(ada0[:, r, k, :], ada0[:, r, k, :], c_act[:, k:k + 1], ada0[:, r, k - 1, :],
                                                   ALU.mult, ALU.add).then_inc(dve_ada, 1)
                if r == 0:
                    dve_rstd(dve, 0)
                if r == 2:
                    lo_u(dve, 0)
                    lo_u(dve, 1)
                dve.wait_ge(ada0_sum, r + 1)
                k = 2 * r
                nc.vector.tensor_tensor(mods[:, KD + k:KD + k + 2], ps[:, B_MOD, KD + k:KD + k + 2], cols[:, KD + k:KD + k + 2],
                                        ALU.add).then_inc(mod0_done, 1)
                nc.vector.tensor_tensor(mods[:, k:k + 2], ps[:, B_MOD, k:k + 2], cols[:, k:k + 2], ALU.add).then_inc(mod0_done, 1)
                dve.wait_ge(mod0_done, 3 * r + 1)
                nc.vector.scalar_tensor_tensor(a_mul[:, 0, k:k + 2], mods[:, KD + k:KD + k + 2], 1.0,
                                               cols[:, R_G1 + k:R_G1 + k + 2], ALU.add, ALU.mult).then_inc(mod0_done, 1)
                dve.wait_ge(mod0_done, 3 * r + 3)
                for kk in range(k, k + 2):
                    dve_scaled(0, kk)
                    if kk:
                        dve_low(dve, 0, kk - 1)
            dve_low(dve, 0, KD - 1)
            pairs(dve, 0, dve_pair)
            dve_down(dve, 0)
            dve_mods(dve)
            dve_h(dve, 1)

            for q in range(4):
                lo_u(dve, U_LAT + q + 2)
            lo_u(dve, U_QKV + 2)
            lo_u(dve, U_QKV + 3)
            dve.wait_ge(lat_psum, 1)
            nc.vector.tensor_scalar(lat_r[:, 0, :], ps[:, 4, :], 1.0 / 256, EPS, ALU.mult, ALU.add).then_inc(lat_dve, 1)
            dve.wait_ge(lat_psum, 2)
            nc.vector.tensor_scalar(lat_r[:, 1, :], ps[:, 6, :], 1.0 / 128, EPS, ALU.mult, ALU.add).then_inc(lat_dve, 1)
            dve.wait_ge(lat_psum, 3)
            nc.vector.tensor_copy(kw[:, :, :], ps[:, 7, 0:QT * 68].rearrange("p (t n) -> p t n", t=QT)).then_inc(lat_dve, 1)
            dve.wait_ge(lat_dve, 3)
            for t in range(QT):
                nc.vector.bn_stats(stats[:, t, :], kw[:, t, 0:64]).then_inc(lat_dve, 1)
            for t in range(QT):
                dve.wait_ge(lat_dve, 4 + t)
                nc.vector.bn_aggr(mean[:, t, :], stats[:, t, :]).then_inc(lat_dve, 1)
            dve.wait_ge(lat_dve, 11)
            nc.vector.tensor_scalar(k_rstd[:, :, 0], mean[:, :, 1], EPS, None, ALU.add).then_inc(lat_dve, 1)
            lo_u(dve, U_QKV + 4)
            dve.wait_ge(lat_act, 3)
            nc.vector.reciprocal(k_rstd[:, :, 1], k_rstd[:, :, 0]).then_inc(lat_dve, 1)
            dve.wait_ge(lat_dve, 13)
            for t in range(QT):
                for half in range(2):
                    last = nc.vector.tensor_scalar(kn[:, t, 64 * half:64 * half + 64], kw[:, t, 0:64], mean[:, t, 0:1],
                                                   k_rstd[:, t, 1:2], ALU.subtract, ALU.mult)
            nc.vector.tensor_copy(widx[:, :, :], kw[:, :, 64:68]).then_inc(lat_dve, 1)
            for r in range(2):
                nc.vector.reciprocal(lat_r[:, r, :], lat_r[:, r, :]).then_inc(lat_dve, 1)
            lo_u(dve, U_QKV + 5)
            dve.wait_ge(lat_dve, 16)
            for r in range(2):
                nc.vector.scalar_tensor_tensor(cq[:, r, :], cq[:, r, :], cols[:, R_CQ + r:R_CQ + r + 1], lat_r[:, 0, :],
                                               ALU.mult, ALU.mult)
            nc.vector.scalar_tensor_tensor(ckv[:, :], ckv[:, :], cols[:, R_CKV:R_CKV + 1], lat_r[:, 1, :],
                                           ALU.mult, ALU.mult).then_inc(lat_dve, 1)
            lo_u(dve, U_QKV + 6)
            lo_u(dve, U_QKV + 7)
            dve.wait_ge(kn_psum, 1)
            nc.vector.tensor_scalar(ki[:, :], ps[:, 7, :], cols[:, R_GK:R_GK + 1], cols[:, R_BK:R_BK + 1],
                                    ALU.mult, ALU.add).then_inc(lat_dve, 1)
            dst = [qi[:, 0, :], qi[:, 1, :]] + [dq[:, r, :] for r in range(HP)] + [dk[:, r, :] for r in range(HP)] \
                + [dv[:, r, :] for r in range(QT)]
            for n in range(14):
                dve.wait_ge(prj_psum, n + 1)
                if 2 <= n < 6:
                    nc.vector.tensor_scalar(dst[n], ps[:, 4 + n % 3, :], HEAD_DIM ** -0.5, None, ALU.mult).then_inc(prj_free, 1)
                else:
                    nc.vector.tensor_copy(dst[n], ps[:, 4 + n % 3, :]).then_inc(prj_free, 1)
            for q in range(6, 12):
                lo_u(dve, U_QKV + q + 2)
            for t in range(QT):
                dve.wait_ge(vt_psum, t + 1)
                nc.vector.tensor_copy(mv[:, t, :], ps[:, (7, 4, 5, 6)[t], :]).then_inc(vt_done, 1)
            n = 0
            for c in range(1, QT):
                w = (c + 1) * P
                for h in range(IDX_HEADS):
                    sc = score[:, c - 1, 0:w]
                    dve.wait_ge(is_relu, n + 1)
                    if h == 0:
                        nc.vector.tensor_scalar(sc, relu[:, n % 3, 0:w], widx[:, c, 0:1], None, ALU.mult).then_inc(is_acc, 1)
                    else:
                        dve.wait_ge(is_acc, n)
                        nc.vector.scalar_tensor_tensor(sc, relu[:, n % 3, 0:w], widx[:, c, h:h + 1], sc,
                                                       ALU.mult, ALU.add).then_inc(is_acc, 1)
                    n += 1
            def select_round(done_before):
                for c in range(3):
                    dve.wait_ge(tk_step, done_before + c)
                    nc.vector.max(max8[:, c, :], score[:, c, 0:(c + 2) * P]).then_inc(tk_step, 1)
                for c in range(3):
                    dve.wait_ge(tk_step, done_before + 3 + c)
                    nc.vector.match_replace(score[:, c, 0:(c + 2) * P], max8[:, c, :], score[:, c, 0:(c + 2) * P],
                                            TAKEN).then_inc(tk_step, 1)

            dve.wait_ge(causal_done, 3)
            for q in range(16):
                lo_u(dve, U_GATE + q + 2)
                select_round(6 * q + 1)
            tk = 3 + 6 * 16
            dve.wait_ge(tk_step, tk)
            dve.wait_ge(dist_done, 2)
            for c in range(3):
                w = (c + 2) * P
                nc.vector.tensor_scalar(score[:, c, 0:w], score[:, c, 0:w], TAKEN, MASKED, ALU.not_equal, ALU.mult)\
                    .then_inc(tk_step, 1)
            for c in range(3):
                w = (c + 2) * P
                dve.wait_ge(tk_step, tk + 1 + c)
                nc.vector.tensor_tensor(score[:, c, 0:w], score[:, c, 0:w], dist[:, SEQ - w:SEQ], ALU.add).then_inc(tk_step, 1)
            dve.wait_ge(tk_step, tk + 6)

            def biased(n):
                b, hp, e, c = steps[n]
                w = (c + 1) * P
                slope = 2.0 ** (-8.0 * (2 * hp + e + 1) / HEADS)
                d = score[:, c - 1, 0:w] if b and c else dist[:, SEQ - w:SEQ]
                dve.wait_ge(s_psum, n + 1)
                if n >= 3:
                    dve.wait_ge(pt_psum, n - 2)
                nc.vector.scalar_tensor_tensor(prob[:, n % 3, 0:w], d, slope, ps[:, B_S[n % 2], 0:w],
                                               ALU.mult, ALU.add).then_inc(s_used, 1)
                dve.wait_ge(s_used, n + 1)
                nc.vector.tensor_reduce(nmax[:, n % 4, :], prob[:, n % 3, 0:w], AX.X, ALU.max, negate=True).then_inc(m_done, 1)

            def normalise(n):
                w = (steps[n][3] + 1) * P
                dve.wait_ge(e_done, n + 1)
                nc.vector.reciprocal(rsum[:, n % 4, :], psumq[:, n % 4, :]).then_inc(r_done, 1)
                dve.wait_ge(r_done, n + 1)
                nc.vector.tensor_scalar(prob[:, n % 3, 0:w], prob[:, n % 3, 0:w], rsum[:, n % 4, :], None,
                                        ALU.mult).then_inc(p_done, 1)

            def o_low(pair):
                dve.wait_ge(ohi_done, pair + 1)
                nc.vector.tensor_tensor(h_lo[:, pair, :], ps[:, B_O[pair % 2], :], h_hi[:, pair, :].bitcast(F32),
                                        ALU.subtract).then_inc(olo_done, 1)

            for n in range(NST + 4):
                if n < NST:
                    biased(n)
                if 1 <= n < NST + 1:
                    normalise(n - 1)
                if n >= 11 and (n - 11) % 8 == 0:
                    o_low((n - 11) // 8)
            for q in range(KD):
                lo_u(dve, U_MERGE + q + 2)
                dve.wait_ge(unit_done, done(U_MERGE + q))
                m = mrg[:, q % 2]
                nc.vector.tensor_tensor(m[:, 0, :], ps[:, 2 * (q % 2), :], gate[:, q, :], ALU.mult).then_inc(mg_free, 1)
                nc.vector.tensor_tensor(m[:, 1, :], ps[:, 2 * (q % 2) + 1, :], gate[:, KD + q, :], ALU.mult).then_inc(mg_free, 1)
                dve.wait_ge(mg_free, 2 * q + 2)
                nc.vector.tensor_tensor(m[:, 2, :], m[:, 0, :], m[:, 1, :], ALU.add).then_inc(mg_y, 1)
                dve.wait_ge(yhi_done, q + 1)
                nc.vector.tensor_tensor(y_lo[:, q, :], m[:, 2, :], y_hi[:, q, :].bitcast(F32), ALU.subtract).then_inc(ylo_done, 1)
            for q in range(KD):
                dve.wait_ge(unit_done, done(U_OUT + q))
                residual(dve, 1, q, q % 4)
                dve_square_sum(dve, 2, q - 1)
                lo_u(dve, U_OUT + q + 2)
            dve_h(dve, 2)
            pairs(dve, 1, dve_pair)
            dve_down(dve, 1)
            dve.wait_ge(sqrt_done, 4)
            nc.vector.reciprocal(rtok[:, :], rtok[:, :]).then_inc(rstd_done, 1)
            dve.wait_ge(rstd_done, 4)
            dve.wait_ge(fin_tok, KD)
            for t in (1, 3):
                nc.vector.tensor_scalar(out_tok[:, t, :], out_tok[:, t, :], rtok[:, t:t + 1], None, ALU.mult).then_inc(fin_dve, 1)

        @block.gpsimd
        def _(pool):
            nc.gpsimd.memset(ident[:, :], 1.0).then_inc(const_step, 1)
            pool.wait_ge(const_step, 1)
            nc.gpsimd.affine_select(out=ident[:, :], in_=ident[:, :], compare_op=ALU.is_equal, fill=0.0, base=0,
                                    pattern=[[-1, P]], channel_multiplier=1).then_inc(const_done, 1)
            def column_tile(a, last_out, step, at_, wait_last=None):
                nc.gpsimd.tensor_tensor(a, a, c_act[:, :].unsqueeze(2).broadcast_to([P, KD, P]), ALU.mult)\
                    .then_inc(step, 1)
                for r, m in enumerate((4, 2)):
                    pool.wait_ge(step, at_ + r + 1)
                    nc.gpsimd.tensor_tensor(a[:, 0:m, :], a[:, 0:m, :], a[:, m:2 * m, :], ALU.add).then_inc(step, 1)
                pool.wait_ge(step, at_ + 3)
                if wait_last is not None:
                    pool.wait_ge(*wait_last)
                return nc.gpsimd.tensor_tensor(last_out, a[:, 0, :], a[:, 1, :], ALU.add)

            pool.wait_ge(cact_done, 1)
            def chunk(i, n, j, arrival):
                pool.wait_ge(ada_in[j], arrival)
                column_tile(ada[:, j], ada_acc[:, j % 2, :], ada_step, 3 * n, (ada_used, n + 1)).then_inc(ada_sum, 1)

            with pool.Fori(0, KF // 2) as i:
                for j in range(4):
                    chunk(i, 4 * i + j, j, 16 * i + 16)
            with pool.Fori(0, KD // 2 - 1) as i:
                for j in range(4):
                    chunk(i, 2 * KF + 4 * i + j, j, 16 * i + (16 * KF // 2 + 16))
            pool.wait_ge(x_done, 2 * KD)
            nc.gpsimd.iota(dist[:, :], pattern=[[1, SEQ]], base=P - SEQ, channel_multiplier=-1,
                           allow_small_or_imprecise_dtypes=True).then_inc(dist_done, 1)
            pool.wait_ge(dist_done, 1)
            nc.gpsimd.affine_select(out=dist[:, :], in_=dist[:, :], compare_op=ALU.is_ge, fill=MASKED, base=SEQ - P,
                                    pattern=[[-1, SEQ]], channel_multiplier=1).then_inc(dist_done, 1)
            for r, src in enumerate((cq[:, 0, :], cq[:, 1, :], ckv[:, :])):
                pool.wait_ge(evac, r + 1)
                nc.gpsimd.tensor_tensor(lat_sq[:, r, :], src, src, ALU.mult).then_inc(lsq_done, 1)
            pool.wait_ge(is_acc, 3 * IDX_HEADS)
            for c in range(1, QT):
                d = score[:, c - 1, c * P:(c + 1) * P]
                nc.gpsimd.affine_select(out=d, in_=d, compare_op=ALU.is_ge, fill=FUTURE, base=0, pattern=[[-1, P]],
                                        channel_multiplier=1).then_inc(causal_done, 1)

_INS = ["x", "c", "w_ada", "b_ada", "g_ffn1", "w1_ffn1", "w3_ffn1", "w2_ffn1", "g_mix", "w_in", "g_cq", "g_ckv",
        "g_kidx", "b_kidx", "w_uq", "w_qidx", "w_uk", "w_uv", "w_proj_dsa", "w_proj_moba", "w_out", "g_ffn2",
        "w1_ffn2", "w3_ffn2", "w2_ffn2", "g_final"]


def kernel(**inputs):
    import numpy as _np
    import concourse.bacc as _bacc
    from concourse import mybir as _mybir
    from concourse.bass_utils import run_bass_kernel_spmd as _run

    nc = _bacc.Bacc("TRN2", target_bir_lowering=False, num_devices=1)
    arrays, args = {}, []
    for name in _INS:
        a = _np.ascontiguousarray(inputs[name])
        arrays[f"in_{name}"] = a
        args.append(nc.dram_tensor(f"in_{name}", a.shape, _mybir.dt.from_np(a.dtype), kind="ExternalInput").ap())
    args.append(nc.dram_tensor("out_x", inputs["x"].shape, _mybir.dt.float32, kind="ExternalOutput").ap())
    build_layer(nc, *args)
    r = _run(nc, [arrays], core_ids=[0])
    return r.results[0]["out_x"]
```

```python
from contextlib import ExitStack

import concourse.bass as bass
from concourse import mybir

F32 = mybir.dt.float32
F32R = mybir.dt.float32r
ALU = mybir.AluOpType
ACT = mybir.ActivationFunctionType
AX = mybir.AxisListType

P = 128
SEQ = 512
D_MODEL = 1024
D_FF = 2816
HEADS = 8
HEAD_DIM = 64
IDX_HEADS = 4
TOPK = 128
EPS = 1e-6
KD = D_MODEL // P
KF = D_FF // P
KH = KF // 2
QT = SEQ // P
HP = HEADS // 2
N_MOD = 9

RAW = 4
SPL = 2

U_UP = [0, 108]
U_DOWN = [44, 152]
U_LAT = 60
U_QKV = 64
U_GATE = 76
U_MERGE = 92
U_OUT = 100
QKV_COL = 452

R_BADA, R_G1, R_GM, R_G2, R_GF, R_CQ, R_CKV, R_C, R_GK, R_BK = 0, 72, 80, 88, 96, 104, 106, 107, 115, 116
N_ROWS = 117

ADA_FIRST = 2 * KD
ADA_GROUPS = 4
MASKED = -1.0e30
FUTURE = -3.0e38
TAKEN = -3.3e38


def build_layer(nc, x_in, c_in, w_ada, b_ada, g_ffn1, w1_ffn1, w3_ffn1, w2_ffn1, g_mix, w_in, g_cq, g_ckv,
                g_kidx, b_kidx, w_uq, w_qidx, w_uk, w_uv, w_proj_dsa, w_proj_moba, w_out, g_ffn2, w1_ffn2,
                w3_ffn2, w2_ffn2, g_final, out):
    ctx = ExitStack()
    with ctx:
        base = -(-nc.sbuf_base // 64) * 64

        def at(name, shape, offset, dt=F32):
            return nc.alloc_sbuf_tensor_at(name, [P] + shape, dt, offset=base + offset)

        raw = [at(f"raw{r}", [KH * P], r * 5632) for r in range(RAW)]
        raw2 = [at(f"raw2_{b}", [KH * 2 * P], b * 2 * 5632) for b in range(2)]
        w_hi = [at(f"w_hi{r}", [KH * P], 22528 + r * 5632, F32R) for r in range(SPL)]
        w_lo = [at(f"w_lo{r}", [KH * P], 33792 + r * 5632, F32R) for r in range(SPL)]
        xT = at("xT", [KD, SEQ], 45056)
        h_hi = at("h_hi", [KD, SEQ], 61440, F32R)
        h_lo = at("h_lo", [KD, SEQ], 77824, F32R)
        big = 94208
        g_hi = at("g_hi", [KF, SEQ], big, F32R)
        g_lo = at("g_lo", [KF, SEQ], big + 45056, F32R)
        tmp = at("tmp", [4, SEQ], big + 90112)
        nrm = at("nrm", [4, SEQ], big + 81920)
        ada = at("ada", [2, KD, 2 * P], big + 98304)
        ada0 = at("ada0", [ADA_GROUPS, KD, 4 * P], big)
        x_tok = at("x_tok", [QT, D_MODEL], big + 98304)
        x_sq = at("x_sq", [QT, D_MODEL], 77824)
        mod_row = at("mod_row", [2, SEQ], big + 65536)
        dq = at("dq", [HP, SEQ], big)
        dk = at("dk", [HP, SEQ], big + 8192)
        dv = at("dv", [QT, SEQ], big + 16384)
        qi = at("qi", [2, SEQ], big + 24576)
        ki = at("ki", [SEQ], big + 28672)
        score = at("score", [3, SEQ], big + 30720)
        dist = at("dist", [SEQ], big + 36864)
        mq = at("mq", [HP, SEQ], big + 38912)
        mk = at("mk", [HP, SEQ], big + 47104)
        mv = at("mv", [QT, SEQ], big + 55296)
        mvT = at("mvT", [HP, SEQ], big + 92160)
        lat_sq = at("lat_sq", [3, SEQ], big + 63488)
        relu = at("relu", [3, SEQ], big + 63488)
        prob = [at(f"prob{i}", [SEQ], big + (63488, 65536, 67584, 110592)[i]) for i in range(4)]
        probT = at("probT", [2, SEQ], big + 69632)
        kw = at("kw", [QT, 68], big + 71680)
        max8 = at("max8", [3, 8], big + 73728)
        gate = [at(f"gate{g}", [SEQ], big + (75776 + 2048 * g if g < KD else 38912 + 2048 * (g - KD))) for g in range(2 * KD)]
        o_hi = [at(f"o_hi{p}", [SEQ], big + (92160 + 2048 * p if p < HP else 55296 + 2048 * (p - HP)), F32R)
                for p in range(2 * HP)]
        o_lo = [at(f"o_lo{p}", [SEQ], big + (100352 + 2048 * p if p < HP else (24576, 26624, 28672, 108544)[p - HP]), F32R)
                for p in range(2 * HP)]
        cq = at("cq", [2, SEQ], big + 75776)
        ckv = at("ckv", [SEQ], big + 79872)
        kiw = at("kiw", [SEQ], big + 81920)
        s_uq = at("s_uq", [2, SEQ], big + 83968)
        s_qidx = at("s_qidx", [2, 256], big + 88064)
        s_uk = at("s_uk", [SEQ], big + 90112)
        s_uv = at("s_uv", [SEQ], big + 92160)
        lat_r = at("lat_r", [2, SEQ], big + 108544)
        kn = at("kn", [QT, P], big + 112640)
        mrg = at("mrg", [2, 3, SEQ], big)
        out_tok = at("out_tok", [QT, D_MODEL], big + 98304)
        fin = at("fin", [2, SEQ], 61440)
        msc = big + 114688
        ident = at("ident", [P], msc)
        ones = at("ones", [P], msc + 512)
        cols = at("cols", [P], msc + 1024)
        rows = at("rows", [P], big + 81920)
        ada_acc = at("ada_acc", [2, P], msc + 1536)
        mods = at("mods", [N_MOD * KD], msc + 2560)
        c_act = at("c_act", [KD], msc + 2880)
        a_mul = at("a_mul", [3, KD], msc + 2944)
        o_mul = at("o_mul", [3, KD], msc + 3072)
        stats = at("stats", [QT, 6], msc + 3200)
        mean = at("mean", [QT, 2], msc + 3328)
        k_rstd = at("k_rstd", [QT, 2], msc + 3392)
        widx = at("widx", [QT, IDX_HEADS], msc + 3456)
        nmax = at("nmax", [4, 1], msc + 3520)
        psumq = at("psumq", [4, 1], msc + 3552)
        rsum = at("rsum", [4, 1], msc + 3584)
        eps = at("eps", [1], msc + 3616)
        warm = at("warm", [1], msc + 3648)
        rtok = at("rtok", [QT], msc + 3680)
        tsum = at("tsum", [QT], msc + 3744)
        lat_rt = at("lat_rt", [2, QT], msc + 3712)

        ps = ctx.enter_context(nc.psum_tensor("ps", [P, 8, SEQ], F32))
        B_SUM, B_MOD = 4, 5

        def sem(name):
            return ctx.enter_context(nc.semaphore(name))

        x_in_done = [sem(f"x_in{t}") for t in range(QT)]
        x_even = sem("x_even")
        s_rows = sem("s_rows")
        raw_in = [sem(f"raw_in{r}") for r in range(RAW)]
        first_in = [sem(f"first_in{r}") for r in range(2)]
        raw2_in = [sem(f"raw2_in{b}") for b in range(2)]
        hi_done = sem("hi_done")
        lo_done = sem("lo_done")
        unit_done = sem("unit_done")
        silu_done = sem("silu_done")
        g_done = sem("g_done")
        ghi_done = sem("ghi_done")
        glo_done = sem("glo_done")
        x_done = sem("x_done")
        tok_sum = sem("tok_sum")
        sq_done = sem("sq_done")
        acc_done = sem("acc_done")
        sum_done = sem("sum_done")
        sqrt_done = sem("sqrt_done")
        diag_done = sem("diag_done")
        row_done = sem("row_done")
        rstd_done = sem("rstd_done")
        u_done = sem("u_done")
        hhi_done = sem("hhi_done")
        hlo_done = sem("hlo_done")
        ada0_in = [[sem(f"ada0_in{r}_{half}") for half in range(2)] for r in range(ADA_GROUPS)]
        ada_in = [sem(f"ada_in{b}") for b in range(2)]
        ada_step = sem("ada_step")
        ada_sum = sem("ada_sum")
        ada_used = sem("ada_used")
        row_psum = sem("row_psum")
        row_copied = sem("row_copied")
        ada0_sum = sem("ada0_sum")
        dve_ada = sem("dve_ada")
        const_done = sem("const_done")
        const_step = sem("const_step")
        mod0_done = sem("mod0_done")
        cols_psum = sem("cols_psum")
        cols_done = sem("cols_done")
        cact_done = sem("cact_done")
        xt_psum = sem("xt_psum")
        mod_done = sem("mod_done")
        evac = sem("evac")
        small_in = sem("small_in")
        lsq_done = sem("lsq_done")
        lat_psum = sem("lat_psum")
        lat_dve = sem("lat_dve")
        lat_act = sem("lat_act")
        lat_diag = sem("lat_diag")
        lat_row = sem("lat_row")
        kn_psum = sem("kn_psum")
        prj_psum = sem("prj_psum")
        prj_free = sem("prj_free")
        is_psum = sem("is_psum")
        is_relu = sem("is_relu")
        is_acc = sem("is_acc")
        vt_psum = sem("vt_psum")
        vt_done = sem("vt_done")
        causal_done = sem("causal_done")
        dist_done = sem("dist_done")
        tk_step = sem("tk_step")
        s_psum = sem("s_psum")
        s_used = sem("s_used")
        m_done = sem("m_done")
        e_done = sem("e_done")
        r_done = sem("r_done")
        p_done = sem("p_done")
        pt_psum = sem("pt_psum")
        pt_done = sem("pt_done")
        pv_done = sem("pv_done")
        ohi_done = sem("ohi_done")
        olo_done = sem("olo_done")
        sg_done = sem("sg_done")
        mg_free = sem("mg_free")
        mg_y = sem("mg_y")
        yhi_done = sem("yhi_done")
        ylo_done = sem("ylo_done")
        fin_done = sem("fin_done")
        fin_psum = sem("fin_psum")
        fin_tok = sem("fin_tok")
        fin_act = sem("fin_act")
        fin_dve = sem("fin_dve")
        s_out = sem("s_out")

        def ktiles(w):
            return w.rearrange("(k p) n -> p k n", p=P)

        w_up = [[ktiles(w1_ffn1[0]), ktiles(w3_ffn1[0])], [ktiles(w1_ffn2[0]), ktiles(w3_ffn2[0])]]
        w_dn = [ktiles(w2_ffn1[0]), ktiles(w2_ffn2[0])]
        w_in_v, w_out_v = ktiles(w_in[0]), ktiles(w_out[0])
        w_pd_v, w_pm_v = ktiles(w_proj_dsa[0]), ktiles(w_proj_moba[0])
        w_ada_v = ktiles(w_ada[0])

        def nk_of(u):
            return KH if U_DOWN[0] <= u < U_LAT or u >= U_DOWN[1] else KD

        N_UNITS = U_DOWN[1] + 2 * KD

        def done(u):
            return u + 1 + SPL

        def split(u):
            return u + 1 + RAW

        def load_unit(sp, u, j, first, second, nk):
            sp.wait_ge(lo_done, split(U_LAT - (2 if j < 2 else 1)) if u < U_LAT + 4 else u + 1)
            dst = raw[j][:, 0:nk * P].rearrange("p (k n) -> p k n", k=nk)
            m = first.shape[1]
            sp.dma_start(dst[:, 0:m], first).then_inc(raw_in[j], 16)
            sp.dma_start(dst[:, m:nk], second).then_inc(raw_in[j], 16)

        def load_cols(sp, u, j, w, col, k0, nk):
            m = nk // 2
            load_unit(sp, u, j, w[:, k0:k0 + m, bass.ds(col, P)], w[:, k0 + m:k0 + nk, bass.ds(col, P)], nk)

        def raw2_view(b, nk):
            return raw2[b][:, 0:nk * 2 * P].rearrange("p (k n) -> p k n", k=nk)

        def load_pair(sp, u, b, w, col, k0, nk):
            sp.wait_ge(lo_done, u - 2 + 1 + RAW)
            sp.dma_start(raw2_view(b, nk), w[:, k0:k0 + nk, bass.ds(col, 2 * P)]).then_inc(raw2_in[b], 16)

        def load_first(sp, j):
            m = (j // 2) * P
            sp.dma_start(raw2_view(j % 2, KD)[:, :, m:m + P], w_up[0][j % 2][:, :, m:m + P])\
                .then_inc(first_in[j] if j < 2 else raw2_in[j - 2], 16)

        def raw_of(f, j, nk):
            if f is None:
                return raw[j][:, 0:nk * P].rearrange("p (k n) -> p k n", k=nk)
            return raw2_view(j % 2, nk)[:, :, (j // 2) * P:(j // 2 + 1) * P]

        def tiles_of(w, nk):
            return w[:, 0:nk * P].rearrange("p (k n) -> p k n", k=nk)

        ROUNDS = U_LAT // 4
        ROUNDS_MIX = (U_UP[1] - U_LAT) // 4

        def split_hi(act, f, u4, j, nk):
            if f is None:
                act.wait_ge(raw_in[j], 32 * (u4 - ROUNDS + 1))
            elif isinstance(u4, int) and u4 == 0 and j < 2:
                act.wait_ge(first_in[j], 16)
            else:
                act.wait_ge(raw2_in[j % 2], 16 * (u4 - (ROUNDS_MIX if f else 0) + 1))
            act.wait_ge(unit_done, 4 * u4 + j + 1)
            nc.scalar.activation(tiles_of(w_hi[j % SPL], nk), raw_of(f, j, nk), ACT.Copy).then_inc(hi_done, 1)

        def split_lo(dve, f, u4, j, nk):
            dve.wait_ge(hi_done, 4 * u4 + j + 1)
            nc.vector.tensor_tensor(tiles_of(w_lo[j % SPL], nk), raw_of(f, j, nk), tiles_of(w_hi[j % SPL], nk).bitcast(F32),
                                    ALU.subtract).then_inc(lo_done, 1)

        def ffn_of(u):
            return 0 if u < U_LAT else 1 if u >= U_UP[1] else None

        def hi_u(act, u):
            if u < N_UNITS:
                split_hi(act, ffn_of(u), u // 4, u % 4, nk_of(u))

        def lo_u(dve, u):
            if u < N_UNITS:
                split_lo(dve, ffn_of(u), u // 4, u % 4, nk_of(u))

        def mm3(bank, j, kk, rhs_hi, rhs_lo, start, stop):
            hi = w_hi[j % SPL][:, kk * P:(kk + 1) * P]
            lo = w_lo[j % SPL][:, kk * P:(kk + 1) * P]
            nc.tensor.matmul(ps[:, bank, :], hi, rhs_hi, start=start, stop=False)
            nc.tensor.matmul(ps[:, bank, :], hi, rhs_lo, start=False, stop=False)
            return nc.tensor.matmul(ps[:, bank, :], lo, rhs_hi, start=False, stop=stop)

        def unit(bank, j, rhs_hi, rhs_lo, nk=KD, k0=0, start=True, stop=True):
            for kk in range(nk):
                last = mm3(bank, j, kk, rhs_hi[:, k0 + kk, :], rhs_lo[:, k0 + kk, :],
                           start and kk == 0, stop and kk == nk - 1)
            return last

        def act_square(act, n, k):
            act.wait_ge(x_done, KD * n + k + 1)
            if k >= 2:
                act.wait_ge(acc_done, 6 * (n - 1) + k - 1)
            nc.scalar.activation(tmp[:, k % 2, :], xT[:, k, :], ACT.Square).then_inc(sq_done, 1)

        def dve_square_sum(dve, n, k):
            if not 1 <= k < KD - 1:
                return
            dve.wait_ge(sq_done, KD * (n - 1) + k + 1)
            if k > 1:
                dve.wait_ge(acc_done, 6 * (n - 1) + k - 1)
            nc.vector.tensor_tensor(tmp[:, 2, :], tmp[:, 2 if k > 1 else 0, :], tmp[:, k % 2, :], ALU.add)\
                .then_inc(acc_done, 1)

        def pe_keep_busy(count):
            for _ in range(count):
                nc.tensor.matmul(ps[:, 7, 0:P], ident[:, :], ones[:, :], start=True, stop=True)

        def pe_token_sums(pe, n):
            pe.wait_ge(acc_done, 6 * n)
            pe.wait_ge(sq_done, KD * n)
            for t in range(QT):
                nc.tensor.matmul(ps[:, B_SUM, t:t + 1], tmp[:, 2, t * P:(t + 1) * P], ones[:, 0:1], start=True, stop=False)
                last = nc.tensor.matmul(ps[:, B_SUM, t:t + 1], tmp[:, (KD - 1) % 2, t * P:(t + 1) * P], ones[:, 0:1],
                                        start=False, stop=True)
            last.then_inc(sum_done, 1)

        def pe_sum(pe, n):
            if n:
                pe_keep_busy(8)
                pe_token_sums(pe, n)
                pe_keep_busy(6)
            pe.wait_ge(diag_done, n + 1)
            nc.tensor.matmul(ps[:, B_SUM, :], ones[:, :], tmp[:, 3, :], start=True, stop=True).then_inc(row_done, 1)
            if n:
                pe_keep_busy(10)

        def act_warm(act, func):
            act.wait_ge(const_done, 2)
            nc.scalar.activation(warm[:, :], eps[:, :], func)

        def act_sqrt(act, n):
            if n:
                act.wait_ge(sum_done, n)
            else:
                act.wait_ge(tok_sum, QT)
            nc.scalar.activation(rtok[:, :], ps[:, B_SUM, 0:QT] if n else tsum[:, :], ACT.Sqrt, bias=eps[:, :], scale=1.0 / D_MODEL)\
                .then_inc(sqrt_done, 1)

        def dve_diag(dve, dst, r, done_sem, count):
            nc.vector.reciprocal(r, r).then_inc(rstd_done, 1)
            dve.wait_ge(rstd_done, count)
            nc.vector.tensor_tensor(dst.rearrange("p (t n) -> p t n", t=QT), ident[:, :].unsqueeze(1).broadcast_to([P, QT, P]),
                                    r.unsqueeze(2).broadcast_to([P, QT, P]), ALU.mult).then_inc(done_sem, 1)

        def dve_rstd(dve, n):
            dve.wait_ge(sqrt_done, n + 1)
            dve_diag(dve, tmp[:, 3, :], rtok[:, :], diag_done, n + 1 + (2 if n > 1 else 0))
            dve.wait_ge(row_done, n + 1)

        def dve_scaled(n, k):
            nc.vector.scalar_tensor_tensor(nrm[:, k % 4, :], ps[:, B_SUM, :], a_mul[:, n, k:k + 1], xT[:, k, :],
                                           ALU.mult, ALU.mult).then_inc(u_done, 1)

        def dve_low(dve, n, k):
            dve.wait_ge(hhi_done, KD * n + k + 1)
            nc.vector.scalar_tensor_tensor(h_lo[:, k, :], nrm[:, k % 4, :], mods[:, 24 * n + k:24 * n + k + 1],
                                           h_hi[:, k, :].bitcast(F32), ALU.add, ALU.subtract).then_inc(hlo_done, 1)

        def dve_h(dve, n):
            dve_rstd(dve, n)
            dve_scaled(n, 0)
            for k in range(1, KD):
                dve_scaled(n, k)
                dve_low(dve, n, k - 1)
            dve_low(dve, n, KD - 1)

        def act_h(act, n):
            act_sqrt(act, n)
            for k in range(KD):
                act.wait_ge(u_done, KD * n + k + 1)
                nc.scalar.activation(h_hi[:, k, :], nrm[:, k % 4, :], ACT.Identity,
                                     bias=mods[:, 24 * n + k:24 * n + k + 1]).then_inc(hhi_done, 1)
            if n == 2:
                act_warm(act, ACT.Silu)

        def load_rows(eng, vectors):
            for r, src in vectors:
                v = src[0].rearrange("(r n) -> r n", n=P)
                eng.dma_start(rows[r:r + v.shape[0], :], v).then_inc(s_rows, 16)

        def sp_ffn(sp, f, first):
            with sp.Fori(first, KF // 2) as i:
                for b in range(2):
                    load_pair(sp, U_UP[f] + 4 * i + b, b, w_up[f][b], i * (2 * P), 0, KD)
            with sp.Fori(0, KD // 2) as i:
                for b in range(2):
                    load_pair(sp, U_DOWN[f] + 4 * i + b, b, w_dn[f], i * (2 * P), b * KH, KH)

        def pe_ada(pe, n, slot):
            pe.wait_ge(ada_sum, n + 1)
            nc.tensor.matmul(ps[:, B_MOD, bass.ds(n + ADA_FIRST, 1)], ada_acc[:, slot, :], ones[:, 0:1],
                             start=True, stop=True).then_inc(ada_used, 1)

        def pe_first_pair(pe, u, ready, at_, bank=0):
            lag = 4
            pe.wait_ge(lo_done, split(u))
            for kk in range(KD + lag):
                for q, k in ((0, kk), (1, kk - lag)):
                    if q == 0 and k < KD:
                        pe.wait_ge(ready, at_ + k + 1)
                    if q == 1 and k == 0:
                        pe.wait_ge(lo_done, split(u + 1))
                    if 0 <= k < KD:
                        last = mm3(bank + q, u + q, k, h_hi[:, k, :], h_lo[:, k, :], k == 0, k == KD - 1)
                        if k == KD - 1:
                            last.then_inc(unit_done, 1)

        def pe_ffn(pe, f):
            def up(i, j):
                pe.wait_ge(lo_done, U_UP[f] + 4 * i + j + 1 + RAW)
                if j % 2 == 0:
                    pe.wait_ge(g_done, KF * f + 2 * i + j // 2 + 1)
                unit(j, j, h_hi, h_lo).then_inc(unit_done, 1)

            pe_first_pair(pe, U_UP[f], hlo_done, KD * 2 * f)
            for j in range(4):
                if j >= 2:
                    up(0, j)
                if f == 0 and j:
                    pe_ada(pe, j - 1, (j - 1) % 2)
            with pe.Fori(1, KF // 2) as i:
                for j in range(4):
                    up(i, j)
                    if f == 0:
                        pe_ada(pe, 4 * i + j - 1, (j - 1) % 2)
            if f == 0:
                pe_ada(pe, 2 * KF - 1, 1)

            def down(i, with_ada, tiles):
                for j in range(4):
                    pe.wait_ge(lo_done, U_DOWN[f] + 4 * i + j + 1 + RAW)
                    if j % 2 == 0:
                        pe.wait_ge(g_done, KF * (f + 1) + 1)
                        pe.wait_ge(x_done, KD * (1 + 2 * f) + 2 * i + j // 2 - 1)
                    pe.wait_ge(glo_done, KF * f + KH * (j % 2 + 1))
                    unit(j // 2, j, g_hi, g_lo, nk=KH, k0=KH * (j % 2), start=j % 2 == 0, stop=j % 2 == 1)\
                        .then_inc(unit_done, 1)
                    if with_ada:
                        pe.wait_ge(mod_done, 1)
                        pe_ada(pe, 2 * KF + 4 * i + j, j % 2)
                    if j in tiles:
                        pe_token_major(pe, 2 * i + j // 2 - 1, (j // 2 + 1) % 2)

            if f == 0:
                with pe.Fori(0, KD // 2 - 1) as i:
                    down(i, True, ())
                down(KD // 2 - 1, False, ())
            else:
                down(0, False, (2,))
                with pe.Fori(1, KD // 2) as i:
                    down(i, False, (0, 2))

        def pe_token_major(pe, d, slot):
            pe.wait_ge(fin_done, d + 1)
            pe.wait_ge(g_done, 2 * KF + 2)
            for t in range(QT):
                last = nc.tensor.transpose(ps[:, 2 + slot, t * P:(t + 1) * P], fin[:, slot, t * P:(t + 1) * P], ident[:, :])
            last.then_inc(fin_psum, 1)

        def act_pair(act, f, i, jp, nk):
            u = U_UP[f] + 4 * i + 2 * jp
            pair = KF * f + 2 * i + jp
            act.wait_ge(unit_done, u + 1 + SPL)
            act.wait_ge(g_done, pair + 1)
            nc.scalar.activation(tmp[:, jp, :], ps[:, 2 * jp, :], ACT.Silu).then_inc(silu_done, 1)
            split_hi(act, f, U_UP[f] // 4 + i + (jp == 1), (2 * jp + 2) % 4, nk)
            split_hi(act, f, U_UP[f] // 4 + i + (jp == 1), (2 * jp + 3) % 4, nk)
            act.wait_ge(g_done, pair + 1 + 2)
            nc.scalar.activation(g_hi[:, bass.ds(2 * i + jp, 1), :], tmp[:, 2 + jp:3 + jp, :],
                                 ACT.Copy).then_inc(ghi_done, 1)
            if f == 0:
                act_ada(act, 4 * i + 2 * jp + 4, jp)

        def act_ada(act, n, b):
            if not isinstance(n, int) or n >= 4:
                act.wait_ge(ada_sum, n - 2)
            act.dma_start(ada[:, b], w_ada_v[:, :, bass.ds(n * P + ADA_FIRST * P, 2 * P)]).then_inc(ada_in[b], 16)

        def dve_pair(dve, f, i, jp, nk):
            pair = KF * f + 2 * i + jp
            for q in (2, 3):
                split_lo(dve, f, U_UP[f] // 4 + i + (jp == 1), (2 * jp + q) % 4, nk)
            dve.wait_ge(silu_done, pair + 1)
            dve.wait_ge(unit_done, U_UP[f] + 4 * i + 2 * jp + 2 + SPL)
            nc.vector.tensor_tensor(tmp[:, 2 + jp, :], tmp[:, jp, :], ps[:, 2 * jp + 1, :],
                                    ALU.mult).then_inc(g_done, 1)
            dve.wait_ge(ghi_done, pair + 1)
            nc.vector.tensor_tensor(g_lo[:, bass.ds(2 * i + jp, 1), :], tmp[:, 2 + jp:3 + jp, :],
                                    g_hi[:, bass.ds(2 * i + jp, 1), :].bitcast(F32), ALU.subtract).then_inc(glo_done, 1)

        def pairs(eng, f, step):
            with eng.Fori(0, KF // 2 - 1) as i:
                step(eng, f, i, 0, KD)
                step(eng, f, i, 1, KD)
            step(eng, f, KF // 2 - 1, 0, KD)
            step(eng, f, KF // 2 - 1, 1, KH)

        def act_down(act, f):
            for d in range(KD):
                hi_u(act, U_DOWN[f] + 2 * d + 2)
                if f == 0 and d < 4:
                    act_ada(act, 2 * KF + 4 + 2 * d, d % 2)
                if d == KD - 1:
                    act_warm(act, ACT.Sqrt)
                act_square(act, 1 + 2 * f, d)
                if f:
                    act_final(act, d)
                hi_u(act, U_DOWN[f] + 2 * d + 3)

        def act_final(act, d):
            if d >= 2:
                act.wait_ge(fin_psum, d - 1)
            nc.scalar.activation(fin[:, d % 2, :], xT[:, d, :], ACT.Copy, scale=cols[:, R_GF + d:R_GF + d + 1])\
                .then_inc(fin_done, 1)
            if d:
                act_token_major(act, d - 1)

        def act_token_major(act, d):
            act.wait_ge(fin_psum, d + 1)
            nc.scalar.activation(out_tok[:, :, d * P:(d + 1) * P], ps[:, 2 + d % 2, :].rearrange("p (t n) -> p t n", t=QT),
                                 ACT.Copy).then_inc(fin_tok, 1)

        def residual(dve, n, d, bank):
            nc.vector.scalar_tensor_tensor(xT[:, d, :], ps[:, bank, :], o_mul[:, n, d:d + 1], xT[:, d, :],
                                           ALU.mult, ALU.add).then_inc(x_done, 1)

        def dve_down(dve, f):
            if f == 0:
                dve_gate(dve)
            for d in range(KD):
                lo_u(dve, U_DOWN[f] + 2 * d + 2)
                dve_square_sum(dve, 1 + 2 * f, d - 1)
                dve.wait_ge(unit_done, done(U_DOWN[f] + 2 * d + 1))
                residual(dve, 2 * f, d, d % 2)
                lo_u(dve, U_DOWN[f] + 2 * d + 3)

        def dve_gate(dve):
            dve.wait_ge(ada_used, 2 + 2 * KF)
            nc.vector.tensor_tensor(mods[:, 16:24], ps[:, B_MOD, 16:24], cols[:, 16:24], ALU.add).then_inc(mod_done, 1)
            dve.wait_ge(mod_done, 1)
            nc.vector.tensor_scalar(o_mul[:, 0, :], mods[:, 16:24], 0.5, 0.5, ALU.mult, ALU.add).then_inc(mod_done, 1)
            dve.wait_ge(mod_done, 2)

        def dve_mods(dve):
            dve.wait_ge(ada_used, 2 + N_MOD * KD - ADA_FIRST)
            nc.vector.tensor_tensor(mods[:, 24:72], ps[:, B_MOD, 24:72], cols[:, 24:72], ALU.add).then_inc(mod_done, 1)
            dve.wait_ge(mod_done, 3)
            nc.vector.tensor_scalar(o_mul[:, 1, :], mods[:, 40:48], 1.0, None, ALU.add).then_inc(mod_done, 1)
            nc.vector.tensor_scalar(o_mul[:, 2, :], mods[:, 64:72], 0.5, 0.5, ALU.mult, ALU.add).then_inc(mod_done, 1)
            for n, r in ((1, R_GM), (2, R_G2)):
                nc.vector.scalar_tensor_tensor(a_mul[:, n, :], mods[:, 24 * n + 8:24 * n + 16], 1.0, cols[:, r:r + KD],
                                               ALU.add, ALU.mult).then_inc(mod_done, 1)
            dve.wait_ge(mod_done, 7)

        steps = [(b, hp, e, c) for b in range(2) for hp in range(HP) for e in range(2) for c in range(QT)]
        NST = len(steps)
        B_S, B_T, B_O = (0, 1), (2, 3), (6, 7)
        OUT_BANK = (2, 3, 0, 1)

        GATE_TILES = 2 * KD * KD
        gate_tiles, given = [], 0
        for n in range(NST + 5):
            take = min(3 if n < 18 else 2 if n < 46 else 1, GATE_TILES - given)
            gate_tiles.append(range(given, given + take))
            given += take
        assert given == GATE_TILES

        def gates_ended(n):
            return [i // KD for i in gate_tiles[n] if i % KD == KD - 1] if 0 <= n < NST + 5 else []

        def mod0_col(r):
            return (KD if r % 2 == 0 else 0) + 4 * (r // 2)

        def mod0_before(r):
            return 3 * (r // 2) + 2 * (r % 2)

        block = ctx.enter_context(nc.Block())

        @block.sync
        def _(sp):
            load_rows(sp, ((R_C, c_in), (R_BADA, b_ada), (R_G1, g_ffn1), (R_GM, g_mix), (R_G2, g_ffn2)))
            for t in range(QT):
                sp.dma_start(x_tok[:, t, :], x_in[0, t * P:(t + 1) * P, :]).then_inc(x_in_done[t], 16)

            def ada_group(r):
                c = (r // 2) * 4 * P + (D_MODEL if r % 2 == 0 else 0)
                for half in range(2):
                    k = half * KD // 2
                    sp.dma_start(ada0[:, r, k:k + KD // 2, :], w_ada_v[:, k:k + KD // 2, c:c + 4 * P])\
                        .then_inc(ada0_in[r][half], 16)

            ada_group(0)
            ada_group(1)
            ada_group(2)
            ada_group(3)
            load_first(sp, 0)
            load_first(sp, 1)
            load_first(sp, 2)
            load_first(sp, 3)
            sp_ffn(sp, 0, 1)
            for q in range(4):
                load_cols(sp, U_LAT + q, q, w_in_v, q * P, 0, KD)
            for q in range(4):
                load_cols(sp, U_QKV + q, q, w_in_v, QKV_COL + q * P, 0, KD)
            sp.wait_ge(unit_done, done(U_LAT - 1))
            sp.dma_start(s_uq[:], w_uq[0].rearrange("(k p) h d -> p k (h d)", p=P)).then_inc(small_in, 16)
            sp.dma_start(s_qidx[:], w_qidx[0].rearrange("(k p) h d -> p k (h d)", p=P)).then_inc(small_in, 16)
            sp.dma_start(s_uk[:], w_uk[0].rearrange("p h d -> p (h d)")).then_inc(small_in, 16)
            sp.dma_start(s_uv[:], w_uv[0].rearrange("p h d -> p (h d)")).then_inc(small_in, 16)
            with sp.Fori(0, 6) as i:
                for j in range(4):
                    load_cols(sp, U_QKV + 4 + 4 * i + j, j, w_in_v, i * (4 * P) + (QKV_COL + (4 + j) * P), 0, KD)
            for q in range(KD):
                load_unit(sp, U_MERGE + q, q % 4, w_pd_v[:, :, q * P:(q + 1) * P], w_pm_v[:, :, q * P:(q + 1) * P], KD)
            for q in range(KD):
                load_cols(sp, U_OUT + q, q % 4, w_out_v, q * P, 0, KD)
            sp_ffn(sp, 1, 0)
            for t in range(QT):
                sp.wait_ge(fin_act if t % 2 == 0 else fin_dve, t // 2 + 1)
                sp.dma_start(out[0, t * P:(t + 1) * P, :], out_tok[:, t, :]).then_inc(s_out, 16)
            sp.wait_ge(s_out, 16 * QT)

        @block.tensor
        def _(pe):
            pe.sem_inc(unit_done, SPL)
            pe.sem_inc(ada_used, 2)
            pe.wait_ge(s_rows, 16 * 12)
            pe.wait_ge(const_done, 2)
            nc.tensor.transpose(ps[:, B_MOD, 0:N_ROWS], rows[0:N_ROWS, :], ident[0:N_ROWS, 0:N_ROWS]).then_inc(cols_psum, 1)
            for t in range(QT):
                pe.wait_ge(x_in_done[t], 16)
            for k in range(KD):
                bank = (0, 1, 2, 3)[k % 4]
                if k >= 4:
                    pe.wait_ge((x_even, x_done)[k % 2], k // 2 - 1)
                for t in range(QT):
                    last = nc.tensor.transpose(ps[:, bank, t * P:(t + 1) * P], x_tok[:, t, k * P:(k + 1) * P], ident[:, :])
                last.then_inc(xt_psum, 1)
            def group_row(r, first, last):
                if r == ADA_GROUPS:
                    return
                if first == KD // 2:
                    pe.wait_ge(ada0_in[r][1], 16)
                for k in range(first, last):
                    nc.tensor.matmul(ps[0:1, 6 + r % 2, :], c_act[:, k:k + 1], ada0[:, r, k, :], start=k == KD // 2, stop=False)

            def group_columns(r):
                pe.wait_ge(dve_ada, KD // 2 * (r + 1))
                nc.tensor.matmul(ps[0:1, 6 + r % 2, :], ones[:, 0:1], ada0[:, r, KD // 2 - 1, :], start=False, stop=True)\
                    .then_inc(row_psum, 1)
                group_row(r + 1, KD // 2, KD // 2 + 1)
                pe.wait_ge(row_copied, r + 1)
                if r:
                    pe.wait_ge(mod0_done, mod0_before(r - 1) + 1)
                for q in range(4):
                    n = mod0_col(r) + q
                    last = nc.tensor.matmul(ps[:, B_MOD, n:n + 1], mod_row[0:1, r % 2, q * P:(q + 1) * P], ones[0:1, 0:1],
                                            start=True, stop=True)
                last.then_inc(ada0_sum, 1)

            pe.wait_ge(cact_done, 1)
            group_row(0, KD // 2, KD)
            pe_sum(pe, 0)
            group_columns(0)
            for r in range(1, ADA_GROUPS):
                group_row(r, KD // 2 + 1, KD)
                group_columns(r)
            pe.wait_ge(mod0_done, mod0_before(ADA_GROUPS))
            pe_ffn(pe, 0)
            pe_sum(pe, 1)

            def single(u):
                pe.wait_ge(lo_done, split(u))
                if u >= U_LAT + 4:
                    pe.wait_ge(evac, u - U_LAT - 3)
                for kk in range(KD):
                    last = mm3(u % 4, u, kk, h_hi[:, kk, :], h_lo[:, kk, :], kk == 0, kk == KD - 1)
                last.then_inc(unit_done, 1)

            pe_first_pair(pe, U_LAT, hlo_done, KD)
            single(U_LAT + 2)
            single(U_LAT + 3)
            single(U_QKV)
            single(U_QKV + 1)
            pe.wait_ge(lsq_done, 3)
            for t in range(QT):
                for r in range(2):
                    nc.tensor.matmul(ps[:, 4, t:t + 1], lat_sq[:, r, t * P:(t + 1) * P], ones[:, 0:1], start=r == 0, stop=r == 1)
                last = nc.tensor.matmul(ps[:, 4, QT + t:QT + t + 1], lat_sq[:, 2, t * P:(t + 1) * P], ones[:, 0:1],
                                        start=True, stop=True)
            last.then_inc(lat_psum, 1)
            pe.wait_ge(evac, 4)
            for t in range(QT):
                last = nc.tensor.transpose(ps[:, 7, t * 68:(t + 1) * 68], kiw[0:68, t * P:(t + 1) * P], ident[0:68, 0:68])
            last.then_inc(lat_psum, 1)
            for q in range(2, 4):
                single(U_QKV + q)
            for r in range(2):
                pe.wait_ge(lat_diag, r + 1)
                nc.tensor.matmul(ps[:, 4 + 2 * r, :], ones[:, :], lat_r[:, r, :], start=True, stop=True).then_inc(lat_row, 1)
            for q in range(4, 6):
                single(U_QKV + q)
            pe.wait_ge(lat_dve, 13)
            for t in range(QT):
                last = nc.tensor.transpose(ps[:, 7, t * P:(t + 1) * P], kn[:, t, :], ident[:, :])
            last.then_inc(kn_psum, 1)
            pe.wait_ge(small_in, 64)
            pe.wait_ge(lat_dve, 14)
            for n in range(14):
                bank = 4 + n % 3
                if n >= 3:
                    pe.wait_ge(prj_free, n - 2)
                if n < 6:
                    for r in range(2):
                        w = s_qidx[:, r, n * P:(n + 1) * P] if n < 2 else s_uq[:, r, (n - 2) * P:(n - 1) * P]
                        last = nc.tensor.matmul(ps[:, bank, :], w, cq[:, r, :], start=r == 0, stop=r == 1)
                elif n < 10:
                    last = nc.tensor.matmul(ps[:, bank, :], s_uk[:, (n - 6) * P:(n - 5) * P], ckv[:, :], start=True, stop=True)
                else:
                    last = nc.tensor.matmul(ps[:, bank, :], ckv[:, (n - 10) * P:(n - 9) * P], s_uv[:, :], start=True, stop=True)
                last.then_inc(prj_psum, 1)
            single(U_QKV + 6)
            pe.wait_ge(prj_free, 14)
            pe.wait_ge(lat_dve, 15)
            n = 0
            for c in range(1, QT):
                for h in range(IDX_HEADS):
                    if n >= 3:
                        pe.wait_ge(is_relu, n - 2)
                    o = 64 * (h % 2)
                    nc.tensor.matmul(ps[:, 4 + n % 3, 0:(c + 1) * P], qi[o:o + 64, h // 2, c * P:(c + 1) * P],
                                     ki[o:o + 64, 0:(c + 1) * P], start=True, stop=True).then_inc(is_psum, 1)
                    n += 1
            for q in range(7, 12):
                single(U_QKV + q)
            def value_tile(t):
                if t == 0:
                    pe.wait_ge(evac, 16)
                if t >= 2:
                    pe.wait_ge(vt_done, t - 1)
                for hp in range(HP):
                    last = nc.tensor.transpose(ps[:, B_O[t % 2], hp * P:(hp + 1) * P], mvT[:, hp, t * P:(t + 1) * P], ident[:, :])
                last.then_inc(vt_psum, 1)

            def gate_tile(i):
                g, kk = i // KD, i % KD
                if kk == 0:
                    pe.wait_ge(lo_done, split(U_GATE + g))
                    if g < 2:
                        pe.wait_ge(is_relu, 3 * IDX_HEADS)
                    else:
                        pe.wait_ge(evac, 16 + g - 1)
                last = mm3(4 + g % 2, g, kk, h_hi[:, kk, :], h_lo[:, kk, :], kk == 0, kk == KD - 1)
                if kk == KD - 1:
                    last.then_inc(unit_done, 1)

            def scores(n):
                b, hp, e, c = steps[n]
                q, k = ((mq, mk), (dq, dk))[b]
                if n >= 2:
                    pe.wait_ge(s_used, n - 1)
                o = 64 * e
                nc.tensor.matmul(ps[:, B_S[n % 2], 0:(c + 1) * P], q[o:o + 64, hp, c * P:(c + 1) * P],
                                 k[o:o + 64, hp, 0:(c + 1) * P], start=True, stop=True).then_inc(s_psum, 1)

            def transposes(n):
                c = steps[n][3]
                pe.wait_ge(p_done, n + 1)
                if n >= 2:
                    pe.wait_ge(pt_done, n - 1)
                for s in range(c + 1):
                    last = nc.tensor.transpose(ps[:, B_T[n % 2], s * P:(s + 1) * P], prob[n % 4][:, s * P:(s + 1) * P], ident[:, :])
                last.then_inc(pt_psum, 1)

            def values(n):
                b, hp, e, c = steps[n]
                v = (mv, dv)[b]
                pair = HP * b + hp
                pe.wait_ge(pt_done, n + 1)
                if n == 0:
                    pe.wait_ge(vt_done, QT)
                if pair >= 2 and e == 0 and c == 0:
                    pe.wait_ge(olo_done, pair - 1)
                for s in range(c + 1):
                    last = nc.tensor.matmul(ps[64 * e:64 * e + 64, B_O[pair % 2], c * P:(c + 1) * P],
                                            v[:, s, hp * P + 64 * e:hp * P + 64 * e + 64], probT[:, n % 2, s * P:(s + 1) * P],
                                            start=s == 0, stop=s == c)
                last.then_inc(pv_done, 1)

            for n in range(NST + 5):
                if n < NST:
                    scores(n)
                for i in gate_tiles[n][:2]:
                    gate_tile(i)
                if 3 <= n < NST + 3:
                    transposes(n - 3)
                for i in gate_tiles[n][2:]:
                    gate_tile(i)
                if n < QT:
                    value_tile(n)
                if 4 <= n < NST + 4:
                    values(n - 4)
            for q in range(KD):
                pe.wait_ge(lo_done, split(U_MERGE + q))
                if q < 2:
                    pe.wait_ge(evac, 31 + q)
                else:
                    pe.wait_ge(mg_free, 2 * (q - 1))
                for half in (1, 0):
                    for kk in range(HP):
                        tile = (1 - half) * HP + kk
                        pe.wait_ge(olo_done, 2 * HP if half == 0 else HP)
                        last = mm3(4 * half + q % 2, q, half * HP + kk, o_hi[tile][:, :], o_lo[tile][:, :], kk == 0, kk == HP - 1)
                last.then_inc(unit_done, 1)
            pe_first_pair(pe, U_OUT, ylo_done, 0, OUT_BANK[0])
            for q in range(2, KD):
                pe.wait_ge(lo_done, split(U_OUT + q))
                if q < 4:
                    pe.wait_ge(mg_free, 2 * KD)
                else:
                    pe.wait_ge(x_done, 2 * KD + q - 3)
                unit(OUT_BANK[q % 4], q, h_hi, h_lo).then_inc(unit_done, 1)
            pe_sum(pe, 2)
            pe_ffn(pe, 1)
            pe_keep_busy(8)
            pe_token_sums(pe, 3)
            pe_token_major(pe, KD - 1, (KD - 1) % 2)

        @block.scalar
        def _(act):
            load_rows(act, ((R_CQ, g_cq), (R_CKV, g_ckv)))
            act.dma_start(rows[R_GF:R_GF + KD, :], g_final.rearrange("(r n) -> r n", n=P)).then_inc(s_rows, 16)
            for r, src in ((R_GK, g_kidx), (R_BK, b_kidx)):
                for half in range(2):
                    act.dma_start(rows[r:r + 1, 64 * half:64 * half + 64], src).then_inc(s_rows, 16)
            act.wait_ge(cols_done, 1)
            nc.scalar.activation(c_act[:, :], cols[:, R_C:R_C + KD], ACT.Silu).then_inc(cact_done, 1)
            for t in range(QT):
                act.wait_ge(x_in_done[t], 16)
                nc.scalar.activation(x_sq[:, t, :], x_tok[:, t, :], ACT.Square,
                                     accum_out=tsum[:, t:t + 1]).then_inc(tok_sum, 1)
            act_sqrt(act, 0)
            for k in range(0, KD, 2):
                act.wait_ge(xt_psum, k + 1)
                nc.scalar.activation(xT[:, k, :], ps[:, k % 4, :], ACT.Copy).then_inc(x_even, 1)
            def row_copy(r):
                act.wait_ge(row_psum, r + 1)
                nc.scalar.activation(mod_row[0:1, r % 2, :], ps[0:1, 6 + r % 2, :], ACT.Copy).then_inc(row_copied, 1)

            row_copy(0)
            row_copy(1)
            for k in range(KD):
                act.wait_ge(u_done, k + 1)
                act.wait_ge(mod0_done, mod0_before(2 if k < 4 else 4))
                nc.scalar.activation(h_hi[:, k, :], nrm[:, k % 4, :], ACT.Identity, bias=mods[:, k:k + 1]).then_inc(hhi_done, 1)
                if k == 3:
                    row_copy(2)
                    hi_u(act, 0)
                    hi_u(act, 1)
                    row_copy(3)
            for b in range(2):
                act_ada(act, 2 * b, b)
            pairs(act, 0, act_pair)
            act_down(act, 0)
            act_h(act, 1)

            def copy_out(u, dst, func=ACT.Copy, scale=1.0):
                act.wait_ge(unit_done, done(u))
                nc.scalar.activation(dst, ps[:, u % 4, :], func, scale=scale).then_inc(evac, 1)

            def relus():
                n = 0
                for c in range(1, QT):
                    for h in range(IDX_HEADS):
                        act.wait_ge(is_psum, n + 1)
                        if n >= 3:
                            act.wait_ge(is_acc, n - 2)
                        nc.scalar.activation(relu[:, n % 3, 0:(c + 1) * P], ps[:, 4 + n % 3, 0:(c + 1) * P], ACT.Relu,
                                             scale=(IDX_HEADS * 64) ** -0.5).then_inc(is_relu, 1)
                        n += 1

            lat = [cq[:, 0, :], cq[:, 1, :], ckv[:, :], kiw[:, :]]
            for q in range(16):
                if q == 11:
                    relus()
                u = U_LAT + q
                hi_u(act, u + 2)
                if q < 4:
                    copy_out(u, lat[q])
                else:
                    hp = (q - 4) % HP
                    dst = (mq, mk, mvT)[(q - 4) // HP]
                    if q == 12:
                        act.wait_ge(prj_psum, 14)
                    copy_out(u, dst[:, hp, :], scale=HEAD_DIM ** -0.5 if q < 8 else 1.0)
                if q == 6:
                    act.wait_ge(lat_psum, 1)
                    for r, width in ((0, 256), (1, P)):
                        nc.scalar.activation(lat_rt[:, r, :], ps[:, 4, r * QT:(r + 1) * QT], ACT.Sqrt, bias=eps[:, :],
                                             scale=1.0 / width).then_inc(lat_act, 1)
                    act.wait_ge(lat_dve, 10)
                    nc.scalar.activation(k_rstd[:, :, 0], k_rstd[:, :, 0], ACT.Sqrt).then_inc(lat_act, 1)
            def exps(n):
                c = steps[n][3]
                act.wait_ge(m_done, n + 1)
                nc.scalar.activation(prob[n % 4][:, 0:(c + 1) * P], prob[n % 4][:, 0:(c + 1) * P], ACT.Exp,
                                     bias=nmax[:, n % 4, :], accum_out=psumq[:, n % 4, :]).then_inc(e_done, 1)

            def copies(n):
                c = steps[n][3]
                act.wait_ge(pt_psum, n + 1)
                if n >= 2:
                    act.wait_ge(pv_done, n - 1)
                nc.scalar.activation(probT[:, n % 2, 0:(c + 1) * P], ps[:, B_T[n % 2], 0:(c + 1) * P], ACT.Copy)\
                    .then_inc(pt_done, 1)

            def o_high(pair):
                act.wait_ge(pv_done, 8 * (pair + 1))
                nc.scalar.activation(o_hi[pair][:, :], ps[:, B_O[pair % 2], :], ACT.Copy).then_inc(ohi_done, 1)

            for n in range(NST + 5):
                if 3 <= n < NST + 3:
                    copies(n - 3)
                if n < NST:
                    exps(n)
                if n >= 12 and (n - 12) % 8 == 0:
                    o_high((n - 12) // 8)
                for g in gates_ended(n - 1):
                    hi_u(act, U_GATE + g + 2)
                    nc.scalar.activation(gate[g][:, :], ps[:, 4 + g % 2, :], ACT.Copy).then_inc(evac, 1)
            def sigmoids(q):
                for g in (q, KD + q):
                    nc.scalar.activation(gate[g][:, :], gate[g][:, :], ACT.Sigmoid).then_inc(sg_done, 1)

            act.wait_ge(evac, 32)
            sigmoids(0)
            for q in range(KD):
                hi_u(act, U_MERGE + q + 2)
                if q < KD - 1:
                    sigmoids(q + 1)
                act.wait_ge(mg_y, q + 1)
                nc.scalar.activation(h_hi[:, q, :], mrg[:, q % 2, 2, :], ACT.Copy).then_inc(yhi_done, 1)
            for q in range(KD):
                if q == KD - 1:
                    act_warm(act, ACT.Sqrt)
                act_square(act, 2, q)
                hi_u(act, U_OUT + q + 2)
            act_h(act, 2)
            pairs(act, 1, act_pair)
            act_down(act, 1)
            act.wait_ge(sum_done, 3)
            nc.scalar.activation(rtok[:, :], ps[:, B_SUM, 0:QT], ACT.Sqrt, bias=eps[:, :], scale=1.0 / D_MODEL)\
                .then_inc(sqrt_done, 1)
            act_token_major(act, KD - 1)
            act.wait_ge(rstd_done, 6)
            act.wait_ge(fin_tok, KD)
            for t in (0, 2):
                nc.scalar.activation(out_tok[:, t, :], out_tok[:, t, :], ACT.Copy, scale=rtok[:, t:t + 1]).then_inc(fin_act, 1)

        @block.vector
        def _(dve):
            dve.sem_inc(lo_done, RAW)
            dve.sem_inc(g_done, 2)
            dve.sem_inc(tk_step, 3)
            nc.vector.memset(eps[:, :], EPS)
            nc.vector.memset(ones[:, :], 1.0).then_inc(const_done, 1)
            dve.wait_ge(cols_psum, 1)
            nc.vector.tensor_copy(cols[:, 0:N_ROWS], ps[:, B_MOD, 0:N_ROWS]).then_inc(cols_done, 1)
            dve.wait_ge(cact_done, 1)
            for k in range(1, KD, 2):
                dve.wait_ge(xt_psum, k + 1)
                nc.vector.tensor_copy(xT[:, k, :], ps[:, k % 4, :]).then_inc(x_done, 1)
            dve.wait_ge(x_even, KD // 2)
            dve.wait_ge(x_done, KD // 2)
            dve.sem_inc(x_done, KD // 2)
            def ada_chain(r):
                dve.wait_ge(ada0_in[r][0], 16)
                nc.vector.tensor_scalar(ada0[:, r, 0, :], ada0[:, r, 0, :], c_act[:, 0:1], None, ALU.mult).then_inc(dve_ada, 1)
                for k in range(1, KD // 2):
                    dve.wait_ge(dve_ada, KD // 2 * r + k)
                    nc.vector.scalar_tensor_tensor(ada0[:, r, k, :], ada0[:, r, k, :], c_act[:, k:k + 1], ada0[:, r, k - 1, :],
                                                   ALU.mult, ALU.add).then_inc(dve_ada, 1)

            def mods0(r):
                dve.wait_ge(ada0_sum, r + 1)
                n, k = mod0_col(r), 4 * (r // 2)
                nc.vector.tensor_tensor(mods[:, n:n + 4], ps[:, B_MOD, n:n + 4], cols[:, n:n + 4], ALU.add).then_inc(mod0_done, 1)
                if r % 2 == 0:
                    dve.wait_ge(mod0_done, mod0_before(r) + 1)
                    nc.vector.scalar_tensor_tensor(a_mul[:, 0, k:k + 4], mods[:, n:n + 4], 1.0,
                                                   cols[:, R_G1 + k:R_G1 + k + 4], ALU.add, ALU.mult).then_inc(mod0_done, 1)
                    dve.wait_ge(mod0_done, mod0_before(r) + 2)
                    for kk in range(k, k + 4):
                        dve_scaled(0, kk)
                else:
                    for kk in range(k, k + 4):
                        dve_low(dve, 0, kk)

            ada_chain(0)
            dve_rstd(dve, 0)
            ada_chain(1)
            mods0(0)
            ada_chain(2)
            mods0(1)
            ada_chain(3)
            mods0(2)
            lo_u(dve, 0)
            lo_u(dve, 1)
            mods0(3)
            pairs(dve, 0, dve_pair)
            dve_down(dve, 0)
            dve_mods(dve)
            dve_h(dve, 1)

            for q in range(4):
                lo_u(dve, U_LAT + q + 2)
            lo_u(dve, U_QKV + 2)
            lo_u(dve, U_QKV + 3)
            dve.wait_ge(lat_psum, 2)
            nc.vector.tensor_copy(kw[:, :, :], ps[:, 7, 0:QT * 68].rearrange("p (t n) -> p t n", t=QT)).then_inc(lat_dve, 1)
            dve.wait_ge(lat_dve, 1)
            for t in range(QT):
                nc.vector.bn_stats(stats[:, t, :], kw[:, t, 0:64]).then_inc(lat_dve, 1)
            for t in range(QT):
                dve.wait_ge(lat_dve, 2 + t)
                nc.vector.bn_aggr(mean[:, t, :], stats[:, t, :]).then_inc(lat_dve, 1)
            dve.wait_ge(lat_dve, 9)
            nc.vector.tensor_scalar(k_rstd[:, :, 0], mean[:, :, 1], EPS, None, ALU.add).then_inc(lat_dve, 1)
            lo_u(dve, U_QKV + 4)
            dve.wait_ge(lat_act, 3)
            for r in range(2):
                dve_diag(dve, lat_r[:, r, :], lat_rt[:, r, :], lat_diag, 3 + r)
            nc.vector.reciprocal(k_rstd[:, :, 1], k_rstd[:, :, 0]).then_inc(lat_dve, 1)
            dve.wait_ge(lat_dve, 11)
            for t in range(QT):
                for half in range(2):
                    last = nc.vector.tensor_scalar(kn[:, t, 64 * half:64 * half + 64], kw[:, t, 0:64], mean[:, t, 0:1],
                                                   k_rstd[:, t, 1:2], ALU.subtract, ALU.mult)
            last.then_inc(lat_dve, 1)
            nc.vector.tensor_copy(widx[:, :, :], kw[:, :, 64:68]).then_inc(lat_dve, 1)
            lo_u(dve, U_QKV + 5)
            dve.wait_ge(lat_row, 2)
            for r in range(2):
                nc.vector.scalar_tensor_tensor(cq[:, r, :], cq[:, r, :], cols[:, R_CQ + r:R_CQ + r + 1], ps[:, 4, :],
                                               ALU.mult, ALU.mult)
            nc.vector.scalar_tensor_tensor(ckv[:, :], ckv[:, :], cols[:, R_CKV:R_CKV + 1], ps[:, 6, :],
                                           ALU.mult, ALU.mult).then_inc(lat_dve, 1)
            lo_u(dve, U_QKV + 6)
            lo_u(dve, U_QKV + 7)
            dve.wait_ge(kn_psum, 1)
            nc.vector.tensor_scalar(ki[:, :], ps[:, 7, :], cols[:, R_GK:R_GK + 1], cols[:, R_BK:R_BK + 1],
                                    ALU.mult, ALU.add).then_inc(lat_dve, 1)
            dst = [qi[:, 0, :], qi[:, 1, :]] + [dq[:, r, :] for r in range(HP)] + [dk[:, r, :] for r in range(HP)] \
                + [dv[:, r, :] for r in range(QT)]
            for n in range(14):
                dve.wait_ge(prj_psum, n + 1)
                if 2 <= n < 6:
                    nc.vector.tensor_scalar(dst[n], ps[:, 4 + n % 3, :], HEAD_DIM ** -0.5, None, ALU.mult).then_inc(prj_free, 1)
                else:
                    nc.vector.tensor_copy(dst[n], ps[:, 4 + n % 3, :]).then_inc(prj_free, 1)
            lo_u(dve, U_QKV + 8)
            n = 0
            for c in range(1, QT):
                w = (c + 1) * P
                for h in range(IDX_HEADS):
                    sc = score[:, c - 1, 0:w]
                    dve.wait_ge(is_relu, n + 1)
                    if h == 0:
                        nc.vector.tensor_scalar(sc, relu[:, n % 3, 0:w], widx[:, c, 0:1], None, ALU.mult).then_inc(is_acc, 1)
                    else:
                        dve.wait_ge(is_acc, n)
                        nc.vector.scalar_tensor_tensor(sc, relu[:, n % 3, 0:w], widx[:, c, h:h + 1], sc,
                                                       ALU.mult, ALU.add).then_inc(is_acc, 1)
                    n += 1
            def select(i):
                for c in range(3):
                    dve.wait_ge(tk_step, 3 * i + 1 + c)
                    row = score[:, c, 0:(c + 2) * P]
                    if i % 2 == 0:
                        nc.vector.max(max8[:, c, :], row).then_inc(tk_step, 1)
                    else:
                        nc.vector.match_replace(row, max8[:, c, :], row, TAKEN).then_inc(tk_step, 1)

            dve.wait_ge(causal_done, 3)
            selected = 0
            for q in range(7, 12):
                for i in range(3):
                    select(selected)
                    selected += 1
                lo_u(dve, U_QKV + q + 2)
            def mask():
                tk = 3 + 6 * 16
                dve.wait_ge(tk_step, tk)
                for c in range(3):
                    w = (c + 2) * P
                    nc.vector.tensor_scalar(score[:, c, 0:w], score[:, c, 0:w], TAKEN, MASKED, ALU.not_equal, ALU.mult)\
                        .then_inc(tk_step, 1)
                for c in range(3):
                    w = (c + 2) * P
                    dve.wait_ge(tk_step, tk + 1 + c)
                    nc.vector.tensor_tensor(score[:, c, 0:w], score[:, c, 0:w], dist[:, SEQ - w:SEQ], ALU.add).then_inc(tk_step, 1)
                dve.wait_ge(tk_step, tk + 6)

            def biased(n):
                b, hp, e, c = steps[n]
                w = (c + 1) * P
                slope = 2.0 ** (-8.0 * (2 * hp + e + 1) / HEADS)
                d = score[:, c - 1, 0:w] if b and c else dist[:, SEQ - w:SEQ]
                dve.wait_ge(s_psum, n + 1)
                if n >= 4:
                    dve.wait_ge(pt_psum, n - 3)
                nc.vector.scalar_tensor_tensor(prob[n % 4][:, 0:w], d, slope, ps[:, B_S[n % 2], 0:w],
                                               ALU.mult, ALU.add).then_inc(s_used, 1)
                dve.wait_ge(s_used, n + 1)
                nc.vector.tensor_reduce(nmax[:, n % 4, :], prob[n % 4][:, 0:w], AX.X, ALU.max, negate=True).then_inc(m_done, 1)

            def normalise(n):
                w = (steps[n][3] + 1) * P
                dve.wait_ge(e_done, n + 1)
                nc.vector.reciprocal(rsum[:, n % 4, :], psumq[:, n % 4, :]).then_inc(r_done, 1)
                dve.wait_ge(r_done, n + 1)
                nc.vector.tensor_scalar(prob[n % 4][:, 0:w], prob[n % 4][:, 0:w], rsum[:, n % 4, :], None,
                                        ALU.mult).then_inc(p_done, 1)

            def o_low(pair):
                dve.wait_ge(ohi_done, pair + 1)
                nc.vector.tensor_tensor(o_lo[pair][:, :], ps[:, B_O[pair % 2], :], o_hi[pair][:, :].bitcast(F32),
                                        ALU.subtract).then_inc(olo_done, 1)

            dve.wait_ge(dist_done, 2)
            for n in range(NST + 5):
                if n == NST // 2:
                    mask()
                if n < NST:
                    biased(n)
                if 1 <= n < NST + 1:
                    normalise(n - 1)
                if n >= 12 and (n - 12) % 8 == 0:
                    o_low((n - 12) // 8)
                if n < QT:
                    dve.wait_ge(vt_psum, n + 1)
                    nc.vector.tensor_copy(mv[:, n, :], ps[:, B_O[n % 2], :]).then_inc(vt_done, 1)
                if selected < 2 * TOPK // 8:
                    select(selected)
                    selected += 1
                for g in gates_ended(n - 1):
                    lo_u(dve, U_GATE + g + 2)
            for q in range(KD):
                lo_u(dve, U_MERGE + q + 2)
                dve.wait_ge(unit_done, done(U_MERGE + q))
                dve.wait_ge(sg_done, 2 * q + 2)
                m = mrg[:, q % 2]
                nc.vector.tensor_tensor(m[:, 0, :], ps[:, q % 2, :], gate[q][:, :], ALU.mult).then_inc(mg_free, 1)
                nc.vector.tensor_tensor(m[:, 1, :], ps[:, 4 + q % 2, :], gate[KD + q][:, :], ALU.mult).then_inc(mg_free, 1)
                dve.wait_ge(mg_free, 2 * q + 2)
                nc.vector.tensor_tensor(m[:, 2, :], m[:, 0, :], m[:, 1, :], ALU.add).then_inc(mg_y, 1)
                dve.wait_ge(yhi_done, q + 1)
                nc.vector.tensor_tensor(h_lo[:, q, :], m[:, 2, :], h_hi[:, q, :].bitcast(F32), ALU.subtract).then_inc(ylo_done, 1)
            for q in range(KD):
                dve_square_sum(dve, 2, q - 1)
                dve.wait_ge(unit_done, done(U_OUT + q))
                residual(dve, 1, q, OUT_BANK[q % 4])
                lo_u(dve, U_OUT + q + 2)
            dve_h(dve, 2)
            pairs(dve, 1, dve_pair)
            dve_down(dve, 1)
            dve.wait_ge(sqrt_done, 4)
            nc.vector.reciprocal(rtok[:, :], rtok[:, :]).then_inc(rstd_done, 1)
            dve.wait_ge(rstd_done, 6)
            dve.wait_ge(fin_tok, KD)
            for t in (1, 3):
                nc.vector.tensor_scalar(out_tok[:, t, :], out_tok[:, t, :], rtok[:, t:t + 1], None, ALU.mult).then_inc(fin_dve, 1)

        @block.gpsimd
        def _(pool):
            nc.gpsimd.memset(ident[:, :], 1.0).then_inc(const_step, 1)
            pool.wait_ge(const_step, 1)
            nc.gpsimd.affine_select(out=ident[:, :], in_=ident[:, :], compare_op=ALU.is_equal, fill=0.0, base=0,
                                    pattern=[[-1, P]], channel_multiplier=1).then_inc(const_done, 1)
            def column_tile(a, last_out, step, at_, wait_last=None):
                nc.gpsimd.tensor_tensor(a, a, c_act[:, :].unsqueeze(2).broadcast_to([P, KD, P]), ALU.mult)\
                    .then_inc(step, 1)
                for r, m in enumerate((4, 2)):
                    pool.wait_ge(step, at_ + r + 1)
                    nc.gpsimd.tensor_tensor(a[:, 0:m, :], a[:, 0:m, :], a[:, m:2 * m, :], ALU.add).then_inc(step, 1)
                pool.wait_ge(step, at_ + 3)
                if wait_last is not None:
                    pool.wait_ge(*wait_last)
                return nc.gpsimd.tensor_tensor(last_out, a[:, 0, :], a[:, 1, :], ALU.add)

            def chunk(i, n, j, arrival):
                pool.wait_ge(ada_in[j // 2], arrival)
                column_tile(ada[:, j // 2, :, (j % 2) * P:(j % 2 + 1) * P], ada_acc[:, j % 2, :], ada_step, 3 * n,
                            (ada_used, n + 1)).then_inc(ada_sum, 1)

            with pool.Fori(0, KF // 2) as i:
                for j in range(4):
                    chunk(i, 4 * i + j, j, 16 * i + 16)
            with pool.Fori(0, KD // 2 - 1) as i:
                for j in range(4):
                    chunk(i, 2 * KF + 4 * i + j, j, 16 * i + (16 * KF // 2 + 16))
            pool.wait_ge(x_done, 2 * KD)
            nc.gpsimd.iota(dist[:, :], pattern=[[1, SEQ]], base=P - SEQ, channel_multiplier=-1,
                           allow_small_or_imprecise_dtypes=True).then_inc(dist_done, 1)
            pool.wait_ge(dist_done, 1)
            nc.gpsimd.affine_select(out=dist[:, :], in_=dist[:, :], compare_op=ALU.is_ge, fill=MASKED, base=SEQ - P,
                                    pattern=[[-1, SEQ]], channel_multiplier=1).then_inc(dist_done, 1)
            for r, src in enumerate((cq[:, 0, :], cq[:, 1, :], ckv[:, :])):
                pool.wait_ge(evac, r + 1)
                nc.gpsimd.tensor_tensor(lat_sq[:, r, :], src, src, ALU.mult).then_inc(lsq_done, 1)
            pool.wait_ge(is_acc, 3 * IDX_HEADS)
            for c in range(1, QT):
                d = score[:, c - 1, c * P:(c + 1) * P]
                nc.gpsimd.affine_select(out=d, in_=d, compare_op=ALU.is_ge, fill=FUTURE, base=0, pattern=[[-1, P]],
                                        channel_multiplier=1).then_inc(causal_done, 1)

_INS = ["x", "c", "w_ada", "b_ada", "g_ffn1", "w1_ffn1", "w3_ffn1", "w2_ffn1", "g_mix", "w_in", "g_cq", "g_ckv",
        "g_kidx", "b_kidx", "w_uq", "w_qidx", "w_uk", "w_uv", "w_proj_dsa", "w_proj_moba", "w_out", "g_ffn2",
        "w1_ffn2", "w3_ffn2", "w2_ffn2", "g_final"]


def kernel(**inputs):
    import numpy as _np
    import concourse.bacc as _bacc
    from concourse import mybir as _mybir
    from concourse.bass_utils import run_bass_kernel_spmd as _run

    nc = _bacc.Bacc("TRN2", target_bir_lowering=False, num_devices=1)
    arrays, args = {}, []
    for name in _INS:
        a = _np.ascontiguousarray(inputs[name])
        arrays[f"in_{name}"] = a
        args.append(nc.dram_tensor(f"in_{name}", a.shape, _mybir.dt.from_np(a.dtype), kind="ExternalInput").ap())
    args.append(nc.dram_tensor("out_x", inputs["x"].shape, _mybir.dt.float32, kind="ExternalOutput").ap())
    build_layer(nc, *args)
    r = _run(nc, [arrays], core_ids=[0])
    return r.results[0]["out_x"]
```
